# Optimizing a Trainium2 kernel written in Bass

```python
import jax, jax.numpy as jnp
from jax import lax
import numpy as np

D_MODEL = 1024
BATCH = 1
SEQ = 256
DEPTH = 2

CHUNK = 64
N_MIXERS = 2
D_FF = 256 * ((8 * D_MODEL // 3 + 255) // 256)
RMS_EPS = 1e-6
L2_EPS = 1e-6
SC_WIDTH = 3
GDN_HEAD_DIM = 128
GDN_K_HEADS = D_MODEL // 128
GDN_V_HEADS = 2 * GDN_K_HEADS
GDN_KEY_DIM = GDN_K_HEADS * GDN_HEAD_DIM
GDN_VAL_DIM = GDN_V_HEADS * GDN_HEAD_DIM
GDN_CONV_WIDTH = 4
GDN_CONV_DIM = 2 * GDN_KEY_DIM + GDN_VAL_DIM
GDN_IN_DIM = GDN_CONV_DIM + GDN_VAL_DIM + 2 * GDN_V_HEADS
N_SC_LAYERS = (DEPTH + 1) // 2
N_GDN_LAYERS = DEPTH // 2
N_NORMS = 6


def rms_norm(x, g):
    xf = x.astype(jnp.float32)
    y = xf * lax.rsqrt(jnp.mean(xf * xf, axis=-1, keepdims=True) + RMS_EPS)
    return (y * g.astype(jnp.float32)).astype(x.dtype)

def causal_depthwise_conv(x, w):
    k, c = w.shape
    return lax.conv_general_dilated(
        x, w[:, None, :].astype(x.dtype), window_strides=(1,), padding=[(k - 1, 0)],
        dimension_numbers=("NWC", "WIO", "NWC"), feature_group_count=c)

def swiglu(x, w_gate_up, w_down):
    gate, up = jnp.split(x @ w_gate_up, 2, axis=-1)
    return (jax.nn.silu(gate) * up) @ w_down

def short_conv_mixer(x, w_in, conv_w, w_out):
    b, c, v = jnp.split(x @ w_in, 3, axis=-1)
    y = b * causal_depthwise_conv(c * v, conv_w)
    return y @ w_out

def l2norm(x):
    return x * lax.rsqrt(jnp.sum(x * x, axis=-1, keepdims=True) + L2_EPS)

def chunk_gated_delta_rule(q, k, v, g, beta):
    bsz, nh, t, dk = q.shape
    dv = v.shape[-1]
    n = t // CHUNK
    q = q * (dk ** -0.5)

    def rs(a):
        return a.reshape(bsz, nh, n, CHUNK, *a.shape[3:])

    q, k, v, g, beta = rs(q), rs(k), rs(v), rs(g), rs(beta)
    g = jnp.cumsum(g, axis=-1)
    k_beta = k * beta[..., None]
    v_beta = v * beta[..., None]
    idx = jnp.arange(CHUNK)
    causal = idx[:, None] >= idx[None, :]
    strict = idx[:, None] > idx[None, :]
    decay = jnp.exp(jnp.where(causal, g[..., :, None] - g[..., None, :], -jnp.inf))
    a = jnp.where(strict, jnp.einsum("bhncd,bhnsd->bhncs", k_beta, k) * decay, 0.0)
    eye = jnp.eye(CHUNK, dtype=q.dtype)
    t_inv = lax.linalg.triangular_solve(eye + a, jnp.broadcast_to(eye, a.shape),
                                        left_side=True, lower=True)
    u = jnp.einsum("bhncs,bhnse->bhnce", t_inv, v_beta)
    w = jnp.einsum("bhncs,bhnsd->bhncd", t_inv, k_beta * jnp.exp(g)[..., None])
    qk = jnp.where(causal, jnp.einsum("bhncd,bhnsd->bhncs", q, k) * decay, 0.0)
    q_g = q * jnp.exp(g)[..., None]
    g_last = g[..., -1]
    k_tail = k * jnp.exp(g_last[..., None] - g)[..., None]

    def step(state, inp):
        q_g_n, qk_n, u_n, w_n, k_tail_n, gl_n = inp
        v_new = u_n - jnp.einsum("bhcd,bhde->bhce", w_n, state)
        o = jnp.einsum("bhcd,bhde->bhce", q_g_n, state) + jnp.einsum("bhcs,bhse->bhce", qk_n, v_new)
        state = state * jnp.exp(gl_n)[..., None, None] + jnp.einsum("bhcd,bhce->bhde", k_tail_n, v_new)
        return state, o

    xs = tuple(jnp.moveaxis(a_, 2, 0) for a_ in (q_g, qk, u, w, k_tail, g_last))
    s0 = jnp.zeros((bsz, nh, dk, dv), dtype=q.dtype)
    _, o = lax.scan(step, s0, xs)
    return jnp.moveaxis(o, 0, 2).reshape(bsz, nh, t, dv)

def gated_deltanet_mixer(x, w_in, conv_w, a_log, dt_bias, norm_w, w_out):
    bsz, t, _ = x.shape
    proj = x @ w_in
    qkv, z, b, a = jnp.split(proj, [GDN_CONV_DIM, GDN_CONV_DIM + GDN_VAL_DIM,
                                    GDN_CONV_DIM + GDN_VAL_DIM + GDN_V_HEADS], axis=-1)
    qkv = jax.nn.silu(causal_depthwise_conv(qkv, conv_w))
    q, k, v = jnp.split(qkv.astype(jnp.float32), [GDN_KEY_DIM, 2 * GDN_KEY_DIM], axis=-1)
    rep = GDN_V_HEADS // GDN_K_HEADS
    q = jnp.repeat(l2norm(q.reshape(bsz, t, GDN_K_HEADS, GDN_HEAD_DIM)), rep, axis=2)
    k = jnp.repeat(l2norm(k.reshape(bsz, t, GDN_K_HEADS, GDN_HEAD_DIM)), rep, axis=2)
    v = v.reshape(bsz, t, GDN_V_HEADS, GDN_HEAD_DIM)
    beta = jax.nn.sigmoid(b.astype(jnp.float32))
    g = -jnp.exp(a_log.astype(jnp.float32)) * jax.nn.softplus(
        a.astype(jnp.float32) + dt_bias.astype(jnp.float32))
    o = chunk_gated_delta_rule(q.transpose(0, 2, 1, 3), k.transpose(0, 2, 1, 3),
                               v.transpose(0, 2, 1, 3), g.transpose(0, 2, 1),
                               beta.transpose(0, 2, 1))
    o = o.transpose(0, 2, 1, 3)
    o = o * lax.rsqrt(jnp.mean(o * o, axis=-1, keepdims=True) + RMS_EPS) * norm_w.astype(jnp.float32)
    o = o * jax.nn.silu(z.astype(jnp.float32).reshape(bsz, t, GDN_V_HEADS, GDN_HEAD_DIM))
    return o.reshape(bsz, t, GDN_VAL_DIM).astype(x.dtype) @ w_out

def first_inputs(seed: int = 0) -> dict:
    key = jax.random.key(seed)
    ks = jax.random.split(key, 16)
    f32 = jnp.float32
    d = D_MODEL
    x = jax.random.normal(ks[0], (BATCH, SEQ, d), f32)
    norm_g = 1.0 + 0.02 * jax.random.normal(ks[1], (DEPTH, N_NORMS, d), f32)
    ffn_w_gate_up = jax.random.normal(ks[2], (DEPTH, 2, d, 2 * D_FF), f32) * d ** -0.5
    ffn_w_down = jax.random.normal(ks[3], (DEPTH, 2, D_FF, d), f32) * D_FF ** -0.5
    sc_w_in = jax.random.normal(ks[4], (N_SC_LAYERS, d, 3 * d), f32) * d ** -0.5
    sc_conv_w = jax.random.normal(ks[5], (N_SC_LAYERS, SC_WIDTH, d), f32) * SC_WIDTH ** -0.5
    sc_w_out = jax.random.normal(ks[6], (N_SC_LAYERS, d, d), f32) * d ** -0.5
    gdn_w_in = jax.random.normal(ks[7], (N_GDN_LAYERS, d, GDN_IN_DIM), f32) * d ** -0.5
    gdn_conv_w = jax.random.normal(ks[8], (N_GDN_LAYERS, GDN_CONV_WIDTH, GDN_CONV_DIM), f32) * GDN_CONV_WIDTH ** -0.5
    gdn_a_log = jnp.log(jax.random.uniform(ks[9], (N_GDN_LAYERS, GDN_V_HEADS), f32, 1.0, 16.0))
    gdn_dt_bias = 1.0 + 0.1 * jax.random.normal(ks[10], (N_GDN_LAYERS, GDN_V_HEADS), f32)
    gdn_norm_w = 1.0 + 0.02 * jax.random.normal(ks[11], (N_GDN_LAYERS, GDN_HEAD_DIM), f32)
    gdn_w_out = jax.random.normal(ks[12], (N_GDN_LAYERS, GDN_VAL_DIM, d), f32) * GDN_VAL_DIM ** -0.5
    return {"x": x, "norm_g": norm_g, "ffn_w_gate_up": ffn_w_gate_up, "ffn_w_down": ffn_w_down,
            "sc_w_in": sc_w_in, "sc_conv_w": sc_conv_w, "sc_w_out": sc_w_out,
            "gdn_w_in": gdn_w_in, "gdn_conv_w": gdn_conv_w, "gdn_a_log": gdn_a_log,
            "gdn_dt_bias": gdn_dt_bias, "gdn_norm_w": gdn_norm_w, "gdn_w_out": gdn_w_out}

def first_block(x, norm_g, ffn_w_gate_up, ffn_w_down, sc_w_in, sc_conv_w, sc_w_out,
              gdn_w_in, gdn_conv_w, gdn_a_log, gdn_dt_bias, gdn_norm_w, gdn_w_out):
    h = x
    for i in range(DEPTH):
        g = norm_g[i]
        ff = swiglu(rms_norm(h, g[0]), ffn_w_gate_up[i, 0], ffn_w_down[i, 0])
        h = h + 0.5 * rms_norm(ff, g[1])
        m_in = rms_norm(h, g[2])
        j = i // N_MIXERS
        if i % N_MIXERS == 0:
            mix = short_conv_mixer(m_in, sc_w_in[j], sc_conv_w[j], sc_w_out[j])
        else:
            mix = gated_deltanet_mixer(m_in, gdn_w_in[j], gdn_conv_w[j], gdn_a_log[j],
                                       gdn_dt_bias[j], gdn_norm_w[j], gdn_w_out[j])
        h = h + rms_norm(mix, g[3])
        ff = swiglu(rms_norm(h, g[4]), ffn_w_gate_up[i, 1], ffn_w_down[i, 1])
        h = h + 0.5 * rms_norm(ff, g[5])
    return h


DEPTH_2 = 1

NSA_HEADS = 8
NSA_KV_HEADS = 2
NSA_HEAD_DIM = 64
NSA_GROUP = NSA_HEADS // NSA_KV_HEADS
NSA_WIDTH = NSA_HEADS * NSA_HEAD_DIM
CMP_BLOCK = 32
CMP_STRIDE = 16
SLC_BLOCK = 64
SLC_TOPK = 16
WINDOW = 512
Q_BLOCK = 128
FORCE_SCORE = 1e4
NEG_INF = -1e30
RWKV_HEADS = 8
RWKV_HEAD_DIM = 64
RWKV_WIDTH = RWKV_HEADS * RWKV_HEAD_DIM
DECAY_RANK = 64
ICLR_RANK = 64
VRES_RANK = 32
GATE_RANK = 128
LNX_EPS = 1e-5 * RWKV_HEAD_DIM
D_FF_2 = 2816
CONV_WIDTH = 3
EPS = 1e-6
NSA_Q_COLS = NSA_WIDTH
NSA_KV_COLS = NSA_KV_HEADS * NSA_HEAD_DIM
NSA_GATE_COLS = NSA_HEADS * 3
RWKV_SPLITS = (RWKV_WIDTH, RWKV_WIDTH, RWKV_WIDTH, DECAY_RANK, ICLR_RANK, GATE_RANK)
RWKV_COLS = sum(RWKV_SPLITS)
MERGE_COLS = 2 * D_MODEL
IN_SPLITS = (NSA_Q_COLS, NSA_KV_COLS, NSA_KV_COLS, NSA_KV_COLS, NSA_KV_COLS, NSA_KV_COLS, NSA_KV_COLS, NSA_GATE_COLS, RWKV_COLS, MERGE_COLS)
IN_COLS = sum(IN_SPLITS)


def _split(z, sizes):
    return jnp.split(z, np.cumsum(sizes)[:-1].tolist(), axis=-1)

def _rms_norm(x, g):
    x32 = x.astype(jnp.float32)
    y = x32 * lax.rsqrt(jnp.mean(x32 * x32, axis=-1, keepdims=True) + EPS)
    return (y * g.astype(jnp.float32)).astype(x.dtype)

def _masked_softmax(s, mask):
    p = jax.nn.softmax(jnp.where(mask, s.astype(jnp.float32), NEG_INF), axis=-1) * mask
    return p.astype(s.dtype)

def _nsa(q, kc, vc, ks, vs, kw, vw, gate_logits, qk_gain, cmp_pe, cmp_w1, cmp_w2):
    B, S, _ = q.shape
    dt = q.dtype
    G, HG, Dh = NSA_KV_HEADS, NSA_GROUP, NSA_HEAD_DIM
    scale = Dh ** -0.5
    qh = _rms_norm(q.reshape(B, S, G, HG, Dh), qk_gain[0]).transpose(0, 2, 3, 1, 4)

    nc = (S - CMP_BLOCK) // CMP_STRIDE + 1
    tok = np.arange(nc)[:, None] * CMP_STRIDE + np.arange(CMP_BLOCK)[None, :]

    def compress(z, pe, w1, w2):
        blocks = z.reshape(B, S, G, Dh)[:, tok] + pe[None, None, :, None, :]
        hid = jax.nn.silu(jnp.einsum('bnlgd,lde->bnge', blocks, w1))
        return jnp.einsum('bnge,ef->bgnf', hid, w2)

    k_cmp = _rms_norm(compress(kc, cmp_pe[0], cmp_w1[0], cmp_w2[0]), qk_gain[1])
    v_cmp = compress(vc, cmp_pe[1], cmp_w1[1], cmp_w2[1])
    cmp_end = jnp.arange(nc) * CMP_STRIDE + CMP_BLOCK - 1

    ns = S // SLC_BLOCK
    n_sel = min(SLC_TOPK, ns)
    k_slc = _rms_norm(ks.reshape(B, S, G, Dh), qk_gain[2]).transpose(0, 2, 1, 3).reshape(B, G, ns, SLC_BLOCK, Dh)
    v_slc = vs.reshape(B, S, G, Dh).transpose(0, 2, 1, 3).reshape(B, G, ns, SLC_BLOCK, Dh)
    n_idx = jnp.arange(nc)[:, None]
    s_idx = jnp.arange(ns)
    overlap = ((n_idx * CMP_STRIDE < (s_idx[None, :] + 1) * SLC_BLOCK)
               & (n_idx * CMP_STRIDE + CMP_BLOCK > s_idx[None, :] * SLC_BLOCK)).astype(jnp.float32)

    pad = ((0, 0), (0, 0), (WINDOW, 0), (0, 0))
    k_win = jnp.pad(_rms_norm(kw.reshape(B, S, G, Dh), qk_gain[3]).transpose(0, 2, 1, 3), pad)
    v_win = jnp.pad(vw.reshape(B, S, G, Dh).transpose(0, 2, 1, 3), pad)

    gates = jax.nn.sigmoid(gate_logits.astype(jnp.float32)).astype(dt)
    gates = gates.reshape(B, S, G, HG, 3).transpose(0, 2, 3, 1, 4)
    bi = jnp.arange(B)[:, None, None, None]
    gi = jnp.arange(G)[None, :, None, None]

    def block(c):
        t0 = c * Q_BLOCK
        t = t0 + jnp.arange(Q_BLOCK)
        qb = lax.dynamic_slice_in_dim(qh, t0, Q_BLOCK, axis=3)
        gb = lax.dynamic_slice_in_dim(gates, t0, Q_BLOCK, axis=3)
        s = jnp.einsum('bghtd,bgnd->bghtn', qb, k_cmp) * scale
        p_cmp = _masked_softmax(s, cmp_end[None, :] <= t[:, None])
        o_cmp = jnp.einsum('bghtn,bgnd->bghtd', p_cmp, v_cmp)
        imp = jnp.einsum('bghtn,ns->bgts', p_cmp.astype(jnp.float32), overlap)
        cur = t // SLC_BLOCK
        forced = (s_idx[None, :] == 0) | (s_idx[None, :] == cur[:, None]) | (s_idx[None, :] == cur[:, None] - 1)
        imp = jnp.where(forced, FORCE_SCORE, imp)
        imp = jnp.where(s_idx[None, :] > cur[:, None], -1.0, imp)
        _, sel = lax.top_k(imp, n_sel)
        k_sel = k_slc[bi, gi, sel].reshape(B, G, Q_BLOCK, n_sel * SLC_BLOCK, Dh)
        v_sel = v_slc[bi, gi, sel].reshape(B, G, Q_BLOCK, n_sel * SLC_BLOCK, Dh)
        pos = (sel[..., None] * SLC_BLOCK + jnp.arange(SLC_BLOCK)).reshape(B, G, Q_BLOCK, n_sel * SLC_BLOCK)
        s = jnp.einsum('bghtd,bgtkd->bghtk', qb, k_sel) * scale
        p_slc = _masked_softmax(s, pos[:, :, None] <= t[:, None])
        o_slc = jnp.einsum('bghtk,bgtkd->bghtd', p_slc, v_sel)
        k_w = lax.dynamic_slice_in_dim(k_win, t0, WINDOW + Q_BLOCK, axis=2)
        v_w = lax.dynamic_slice_in_dim(v_win, t0, WINDOW + Q_BLOCK, axis=2)
        kpos = t0 - WINDOW + jnp.arange(WINDOW + Q_BLOCK)
        dist = t[:, None] - kpos[None, :]
        s = jnp.einsum('bghtd,bgkd->bghtk', qb, k_w) * scale
        p_win = _masked_softmax(s, (kpos[None, :] >= 0) & (dist >= 0) & (dist < WINDOW))
        o_win = jnp.einsum('bghtk,bgkd->bghtd', p_win, v_w)
        return gb[..., 0:1] * o_cmp + gb[..., 1:2] * o_slc + gb[..., 2:3] * o_win

    o = lax.map(block, jnp.arange(S // Q_BLOCK))
    return o.transpose(1, 0, 4, 2, 3, 5).reshape(B, S, NSA_WIDTH)

def _wkv7_scan(r, w, k, v, a, b):
    B, S, H, N = r.shape

    def step(state, inp):
        r_t, w_t, k_t, v_t, a_t, b_t = inp
        sa = jnp.einsum('bhvk,bhk->bhv', state, a_t)
        state = state * w_t[:, :, None, :] + sa[..., None] * b_t[:, :, None, :] + v_t[..., None] * k_t[:, :, None, :]
        return state, jnp.einsum('bhvk,bhk->bhv', state, r_t)

    xs = (jnp.swapaxes(r, 0, 1), jnp.swapaxes(w, 0, 1), jnp.swapaxes(k, 0, 1),
          jnp.swapaxes(v, 0, 1), jnp.swapaxes(a, 0, 1), jnp.swapaxes(b, 0, 1))
    _, y = lax.scan(step, jnp.zeros((B, H, N, N), jnp.float32), xs)
    return jnp.swapaxes(y, 0, 1)

def _rwkv7(z, v_first, vres, mu, w0, w_up, a0, a_up, g_up, k_k, k_a, r_k, ln_w, ln_b):
    B, S, _ = z.shape
    dt = z.dtype
    f32 = jnp.float32
    H, N = RWKV_HEADS, RWKV_HEAD_DIM
    z_prev = jnp.pad(z[:, :-1], ((0, 0), (1, 0), (0, 0)))
    z = z + mu * (z_prev - z)
    r, k, v, wd, ad, gd = _split(z, RWKV_SPLITS)
    if vres is None:
        v_first = v
    else:
        v0, v1, v2 = vres
        v = v + (v_first - v) * jax.nn.sigmoid(v0 + (v @ v1) @ v2)
    w = -jax.nn.softplus(-(w0 + jnp.tanh(wd) @ w_up).astype(f32)) - 0.5
    decay = jnp.exp(-jnp.exp(w))
    a = jax.nn.sigmoid((a0 + ad @ a_up).astype(f32))
    g = jax.nn.sigmoid(gd) @ g_up

    def heads(t):
        return t.astype(f32).reshape(B, S, H, N)

    rh, vh, ah, wh = heads(r), heads(v), heads(a), heads(decay)
    kk = heads(k * k_k)
    kk = kk / jnp.maximum(jnp.sqrt(jnp.sum(kk * kk, axis=-1, keepdims=True)), 1e-12)
    kh = heads(k) * (1.0 + (ah - 1.0) * k_a.astype(f32).reshape(H, N))
    y = _wkv7_scan(rh, wh, kh, vh, -kk, kk * ah)
    mean = jnp.mean(y, axis=-1, keepdims=True)
    var = jnp.mean(jnp.square(y - mean), axis=-1, keepdims=True)
    y = (y - mean) * lax.rsqrt(var + LNX_EPS) * ln_w.astype(f32).reshape(H, N) + ln_b.astype(f32).reshape(H, N)
    y = y + jnp.sum(rh * kh * r_k.astype(f32), axis=-1, keepdims=True) * vh
    return y.reshape(B, S, RWKV_WIDTH).astype(dt) * g, v_first

def _conv_ffn(h, w_up, conv_w, w_down):
    u = h @ w_up
    u = lax.conv_general_dilated(u, conv_w[:, None, :], window_strides=(1,),
                                 padding=((CONV_WIDTH - 1, 0),),
                                 dimension_numbers=('NWC', 'WIO', 'NWC'),
                                 feature_group_count=u.shape[-1])
    a, b = jnp.split(u, 2, axis=-1)
    return (jax.nn.silu(a) * b) @ w_down

def second_inputs(seed: int = 0) -> dict:
    key = jax.random.key(seed)
    k = jax.random.split(key, 32)
    L, D, Dh = DEPTH_2, D_MODEL, NSA_HEAD_DIM
    f32 = jnp.float32

    def nrm(kk, shape, scale):
        return jax.random.normal(kk, shape, f32) * scale

    def gain(kk, shape):
        return 1.0 + 0.1 * jax.random.normal(kk, shape, f32)

    return {
        'x': nrm(k[0], (BATCH, SEQ, D), 1.0),
        'norm_mix': gain(k[1], (L, D)),
        'norm_ffn': gain(k[2], (L, D)),
        'w_in': nrm(k[3], (L, D, IN_COLS), D ** -0.5),
        'qk_gain': gain(k[4], (L, 4, Dh)),
        'cmp_pe': nrm(k[5], (L, 2, CMP_BLOCK, Dh), 0.1),
        'cmp_w1': nrm(k[6], (L, 2, CMP_BLOCK, Dh, Dh), (CMP_BLOCK * Dh) ** -0.5),
        'cmp_w2': nrm(k[7], (L, 2, Dh, Dh), Dh ** -0.5),
        'rwkv_mu': jax.random.uniform(k[8], (L, RWKV_COLS), f32),
        'rwkv_w0': jax.random.uniform(k[9], (L, RWKV_WIDTH), f32, -3.0, 2.0),
        'rwkv_w_up': nrm(k[10], (L, DECAY_RANK, RWKV_WIDTH), 0.1),
        'rwkv_a0': nrm(k[11], (L, RWKV_WIDTH), 0.5),
        'rwkv_a_up': nrm(k[12], (L, ICLR_RANK, RWKV_WIDTH), ICLR_RANK ** -0.5),
        'rwkv_g_up': nrm(k[13], (L, GATE_RANK, RWKV_WIDTH), GATE_RANK ** -0.5),
        'rwkv_k_k': 0.85 + 0.1 * jax.random.normal(k[14], (L, RWKV_WIDTH), f32),
        'rwkv_k_a': gain(k[15], (L, RWKV_WIDTH)),
        'rwkv_r_k': nrm(k[16], (L, RWKV_HEADS, RWKV_HEAD_DIM), 0.1),
        'rwkv_ln_w': gain(k[17], (L, RWKV_WIDTH)),
        'rwkv_ln_b': nrm(k[18], (L, RWKV_WIDTH), 0.02),
        'vres_v0': nrm(k[19], (L - 1, RWKV_WIDTH), 0.5),
        'vres_v1': nrm(k[20], (L - 1, RWKV_WIDTH, VRES_RANK), RWKV_WIDTH ** -0.5),
        'vres_v2': nrm(k[21], (L - 1, VRES_RANK, RWKV_WIDTH), VRES_RANK ** -0.5),
        'proj_nsa': nrm(k[22], (L, NSA_WIDTH, D), NSA_WIDTH ** -0.5),
        'proj_rwkv': nrm(k[23], (L, RWKV_WIDTH, D), RWKV_WIDTH ** -0.5),
        'w_out': nrm(k[24], (L, D, D), D ** -0.5),
        'ffn_up': nrm(k[25], (L, D, 2 * D_FF_2), D ** -0.5),
        'ffn_conv': nrm(k[26], (L, CONV_WIDTH, 2 * D_FF_2), CONV_WIDTH ** -0.5),
        'ffn_down': nrm(k[27], (L, D_FF_2, D), D_FF_2 ** -0.5),
    }

def second_block(x, norm_mix, norm_ffn, w_in, qk_gain, cmp_pe, cmp_w1, cmp_w2, rwkv_mu, rwkv_w0,
              rwkv_w_up, rwkv_a0, rwkv_a_up, rwkv_g_up, rwkv_k_k, rwkv_k_a, rwkv_r_k, rwkv_ln_w,
              rwkv_ln_b, vres_v0, vres_v1, vres_v2, proj_nsa, proj_rwkv, w_out, ffn_up, ffn_conv,
              ffn_down):
    B, S, D = x.shape
    v_first = None
    for l in range(DEPTH_2):
        h = _rms_norm(x, norm_mix[l])
        u = h @ w_in[l]
        q, kc, vc, ks, vs, kw, vw, nsa_gl, rw, merge = _split(u, IN_SPLITS)
        o_nsa = _nsa(q, kc, vc, ks, vs, kw, vw, nsa_gl, qk_gain[l], cmp_pe[l], cmp_w1[l], cmp_w2[l])
        vres = None if l == 0 else (vres_v0[l - 1], vres_v1[l - 1], vres_v2[l - 1])
        o_rwkv, v_first = _rwkv7(rw, v_first, vres, rwkv_mu[l], rwkv_w0[l], rwkv_w_up[l], rwkv_a0[l],
                                 rwkv_a_up[l], rwkv_g_up[l], rwkv_k_k[l], rwkv_k_a[l], rwkv_r_k[l],
                                 rwkv_ln_w[l], rwkv_ln_b[l])
        gates = jax.nn.sigmoid(merge.astype(jnp.float32)).astype(x.dtype).reshape(B, S, 2, D)
        y = gates[:, :, 0] * (o_nsa @ proj_nsa[l]) + gates[:, :, 1] * (o_rwkv @ proj_rwkv[l])
        x = x + y @ w_out[l]
        x = x + _conv_ffn(_rms_norm(x, norm_ffn[l]), ffn_up[l], ffn_conv[l], ffn_down[l])
    return x


def setup_inputs(seed=0):
    out = dict(first_inputs(seed))
    for name, value in second_inputs(seed + 1).items():
        if name != "x":
            out[name + "_2"] = value
    return out


def reference(
    x, norm_g, ffn_w_gate_up, ffn_w_down, sc_w_in, sc_conv_w, sc_w_out, gdn_w_in, gdn_conv_w,
    gdn_a_log, gdn_dt_bias, gdn_norm_w, gdn_w_out, norm_mix_2, norm_ffn_2, w_in_2, qk_gain_2,
    cmp_pe_2, cmp_w1_2, cmp_w2_2, rwkv_mu_2, rwkv_w0_2, rwkv_w_up_2, rwkv_a0_2, rwkv_a_up_2,
    rwkv_g_up_2, rwkv_k_k_2, rwkv_k_a_2, rwkv_r_k_2, rwkv_ln_w_2, rwkv_ln_b_2, vres_v0_2,
    vres_v1_2, vres_v2_2, proj_nsa_2, proj_rwkv_2, w_out_2, ffn_up_2, ffn_conv_2, ffn_down_2,
):
    x = first_block(
        x, norm_g, ffn_w_gate_up, ffn_w_down, sc_w_in, sc_conv_w, sc_w_out, gdn_w_in,
        gdn_conv_w, gdn_a_log, gdn_dt_bias, gdn_norm_w, gdn_w_out,
    )
    return second_block(
        x, norm_mix_2, norm_ffn_2, w_in_2, qk_gain_2, cmp_pe_2, cmp_w1_2, cmp_w2_2, rwkv_mu_2,
        rwkv_w0_2, rwkv_w_up_2, rwkv_a0_2, rwkv_a_up_2, rwkv_g_up_2, rwkv_k_k_2, rwkv_k_a_2,
        rwkv_r_k_2, rwkv_ln_w_2, rwkv_ln_b_2, vres_v0_2, vres_v1_2, vres_v2_2, proj_nsa_2,
        proj_rwkv_2, w_out_2, ffn_up_2, ffn_conv_2, ffn_down_2,
    )


_drawn_inputs = setup_inputs


def setup_inputs(seed=0):
    import zlib

    import numpy as np

    out = dict(_drawn_inputs(seed))
    spreads = {}
    factors = {'gdn_dt_bias': 53.976,
     'gdn_norm_w': 4.634,
     'qk_gain_2': 8.0,
     'cmp_pe_2': 7.28,
     'rwkv_w_up_2': 4.495,
     'rwkv_k_k_2': 34.162,
     'rwkv_k_a_2': 3.441,
     'rwkv_ln_w_2': 3.864,
     'rwkv_ln_b_2': 23.71,
     'gdn_a_log': 8.0}
    for name, (base, spread) in spreads.items():
        noise = np.random.default_rng([zlib.crc32(name.encode()), seed]).standard_normal(out[name].shape)
        drawn = base * np.exp(spread * noise) if base else spread * noise
        out[name] = __import__('jax').numpy.asarray(drawn.astype(out[name].dtype))
    for name, factor in factors.items():
        out[name] = (out[name] * factor).astype(out[name].dtype)
    return out
```

```python
from contextlib import ExitStack

import numpy as np
import concourse.bass as bass
from concourse import mybir

F32 = mybir.dt.float32
F32R = mybir.dt.float32r
ALU = mybir.AluOpType
ACT = mybir.ActivationFunctionType
AX = mybir.AxisListType

P = 128
SEQ = 256
TB = SEQ // P
D = 1024
DC = D // P
D_FF = 2816
FC = D_FF // P
EPS = 1e-6
HEAD = 128
KH, VH = 8, 16
CONV = 4096
ROWS = 4
RING = 4
GW = 512


def column_rows(ins):
    def rows(ap):
        return ap

    a = [("norm_g", ins["norm_g"].rearrange("l n (c p) -> (l n c) p", p=P), 96),
         ("sc_conv", ins["sc_conv_w"].rearrange("l w (c p) -> (l w c) p", p=P), 24),
         ("norm_mix", ins["norm_mix_2"].rearrange("l (c p) -> (l c) p", p=P), 8)]
    b = [("gdn_conv", ins["gdn_conv_w"].rearrange("l w (c p) -> (l w c) p", p=P), 128)]
    fc = ins["ffn_conv_2"].rearrange("l w (c p) -> (l w c) p", p=P)
    c = [("ffn_conv", fc[0:128], 128)]
    d = [("ffn_conv_end", fc[128:132], 4),
         ("norm_ffn", ins["norm_ffn_2"].rearrange("l (c p) -> (l c) p", p=P), 8),
         ("mu", ins["rwkv_mu_2"].rearrange("l (c p) -> (l c) p", p=P), 14)]
    for n in ("w0", "a0", "k_k", "k_a", "ln_w", "ln_b"):
        d.append((n, ins[f"rwkv_{n}_2"].rearrange("l (c p) -> (l c) p", p=P), 4))
    d.append(("r_k", ins["rwkv_r_k_2"].rearrange("l (c h) p -> (l c) (h p)", h=2), 4))
    d.append(("gdn_norm", ins["gdn_norm_w"], 1))
    e = [("cmp_pe", ins["cmp_pe_2"].rearrange("l c r d -> (l c r) d"), 64),
         ("qk_gain", ins["qk_gain_2"].rearrange("l n d -> (l n) d"), 4)]
    return [a, b, c, d, e]


def weight_groups(ins):
    g = []

    def halves(name, w, off, step, n, piece, k):
        for j in range(n):
            g.append((name, w, [off + j * piece, off + step + j * piece], piece, k))

    def plain(name, w, off, width, k):
        at = off
        while at < off + width:
            n = min(GW, off + width - at)
            g.append((name, w, [at], n, k))
            at += n

    for i in range(2):
        halves(f"ffn{i}0_up", ins["ffn_w_gate_up"][i, 0], 0, D_FF, FC // 2, 256, DC)
        plain(f"ffn{i}0_down", ins["ffn_w_down"][i, 0], 0, D, FC)
        if i == 0:
            halves("sc_cv", ins["sc_w_in"][0], D, D, 4, 256, DC)
            plain("sc_b", ins["sc_w_in"][0], 0, D, DC)
            plain("sc_out", ins["sc_w_out"][0], 0, D, DC)
        else:
            plain("gdn_ba", ins["gdn_w_in"][0], CONV + 2048, 2 * VH, DC)
            plain("gdn_qkv", ins["gdn_w_in"][0], 0, CONV, DC)
            plain("gdn_z", ins["gdn_w_in"][0], CONV, 2048, DC)
            plain("gdn_out", ins["gdn_w_out"][0], 0, D, 2 * DC)
        halves(f"ffn{i}1_up", ins["ffn_w_gate_up"][i, 1], 0, D_FF, FC // 2, 256, DC)
        plain(f"ffn{i}1_down", ins["ffn_w_down"][i, 1], 0, D, FC)
    w = ins["w_in_2"][0]
    plain("mix_q", w, 0, 512, DC)
    plain("mix_kv", w, 512, 512, DC)
    plain("mix_kvg", w, 1024, 280, DC)
    plain("mix_rw", w, 1304, 1792, DC)
    plain("mix_merge", w, 3096, 2048, DC)
    for j in range(2):
        plain(f"mix_pn{j}", ins["proj_nsa_2"][0], j * GW, GW, 4)
        plain(f"mix_pr{j}", ins["proj_rwkv_2"][0], j * GW, GW, 4)
    plain("mix_out", ins["w_out_2"][0], 0, D, DC)
    halves("ffn2_up", ins["ffn_up_2"][0], 0, D_FF, FC // 2, 256, DC)
    plain("ffn2_down", ins["ffn_down_2"][0], 0, D, FC)
    return g


MIX_ORDER = {
    "pe": [
        "hid", "kvc", "kcss", "csc", ("sc", 0), ("sc", 1), ("PT", 0), ("sc", 2), ("PT", 1), ("pv", 0),
        ("sc", 3), ("PT", 2), ("pv", 1), ("sc", 4), ("PT", 3), ("pv", 2), ("sc", 5), ("PT", 4), ("pv", 3),
        ("sc", 6), ("PT", 5), ("pv", 4), ("sc", 7), ("PT", 6), ("pv", 5), ("PT", 7), ("pv", 6), ("pv", 7),
        ("low_rank", 0), ("low_rank", 1), ("low_rank", 2), "kss", "krb", "bon", ("tm", 0, 0), ("tm", 0, 1),
        ("tm", 1, 0), ("tm", 1, 1), ("tm", 2, 0), ("tm", 2, 1), ("gram", 0), ("gv", 0), ("kv", 0),
        ("TN", 0, 0), ("bSA", 0, 0), ("aM", 0, 1), ("TN", 0, 1), ("bSA", 0, 1), ("Y", 0, 0), ("aM", 0, 2),
        ("TN", 0, 2), ("bSA", 0, 2), ("aM", 0, 3), ("TN", 0, 3), ("Y", 0, 1), ("gram", 1), ("gv", 1),
        ("kv", 1), ("TN", 1, 0), ("bSA", 1, 0), ("aM", 1, 1), ("TN", 1, 1), ("bSA", 1, 1), ("Y", 1, 0),
        ("aM", 1, 2), ("TN", 1, 2), ("bSA", 1, 2), ("aM", 1, 3), ("TN", 1, 3), ("Y", 1, 1), "yt",
    ],
    "act": [
        ("qsq", 0), ("qsq", 1), ("ksq", 0), ("ksq", 1), ("wsq", 0), ("wsq", 1), ("gate", 0), ("gate", 1),
        "ksf", ("shift", 0), ("shift", 1), ("shift", 2), ("shift", 3), ("shift", 4), ("shift", 5),
        ("shift", 6), ("shift", 7), ("shift", 8), ("shift", 9), ("shift", 10), ("shift", 11), ("shift", 12),
        ("shift", 13), "hs", "kcs", "kcq", "vc", ("ex", 0, 0, 0), ("ex", 0, 0, 1), ("ex", 0, 1, 0),
        ("ex", 0, 1, 1), "cexp", ("ex", 1, 0, 0), ("ex", 1, 0, 1), ("ex", 1, 1, 0), ("ex", 1, 1, 1),
        ("PTb", 0, 0), ("PTb", 0, 1), ("PT", 0), ("ex", 2, 0, 0), ("ex", 2, 0, 1), ("ex", 2, 1, 0),
        ("ex", 2, 1, 1), ("PTb", 1, 0), ("PTb", 1, 1), ("PT", 1), ("ex", 3, 0, 0), ("ex", 3, 0, 1),
        ("ex", 3, 1, 0), ("ex", 3, 1, 1), ("PTb", 2, 0), ("PTb", 2, 1), ("PT", 2), ("ex", 4, 0, 0),
        ("ex", 4, 0, 1), ("ex", 4, 1, 0), ("ex", 4, 1, 1), ("PTb", 3, 0), ("PTb", 3, 1), ("PT", 3),
        ("ex", 5, 0, 0), ("ex", 5, 0, 1), ("ex", 5, 1, 0), ("ex", 5, 1, 1), ("PTb", 4, 0), ("PTb", 4, 1),
        ("PT", 4), ("ex", 6, 0, 0), ("ex", 6, 0, 1), ("ex", 6, 1, 0), ("ex", 6, 1, 1), ("PTb", 5, 0),
        ("PTb", 5, 1), ("PT", 5), ("ex", 7, 0, 0), ("ex", 7, 0, 1), ("ex", 7, 1, 0), ("ex", 7, 1, 1),
        ("PTb", 6, 0), ("PTb", 6, 1), ("PT", 6), ("PTb", 7, 0), ("PTb", 7, 1), ("PT", 7), ("on", 0),
        ("on", 1), "tw", "sgd", ("sig", 0, 0), ("sig", 0, 1), ("sig", 0, 2), ("sig", 0, 3), ("sig", 1, 0),
        ("sig", 1, 1), ("sig", 1, 2), ("sig", 1, 3), ("kk", 0), ("kk", 1), ("kk", 2), ("kk", 3), "kksq",
        ("g", 0), ("g", 1), "cw", "icw", "cwp", ("tm", 0, 0), ("tm", 0, 1), ("tm", 1, 0), ("tm", 1, 1),
        ("tm", 2, 0), ("tm", 2, 1), ("A", 0, 0), ("A", 0, 1), ("RM", 0, 1, 0), ("RM", 0, 1),
        ("RM", 0, 2, 0), ("RM", 0, 2), ("RM", 0, 3, 0), ("RM", 0, 3), ("A", 1, 0), ("A", 1, 1),
        ("RM", 1, 1, 0), ("RM", 1, 1), ("RM", 1, 2, 0), ("RM", 1, 2), ("RM", 1, 3, 0), ("RM", 1, 3), "ysq",
        ("yf", 0), ("yf", 1), ("yf", 2), ("yf", 3), "on_high", "or_high", ("y_high", 0), ("y_high", 1),
        ("y_high", 2), ("y_high", 3),
    ],
    "dve": [
        "omm", "blk0", "i64_0", "w2a", "w2b", "blk1", "blk", "i64", "qred", "qms", ("qn", 0), ("qn", 1),
        "w1a", "w1b", "kred", "kms", ("kn", 0, 0), ("kn", 0, 1), ("kn", 1, 0), "kn", ("zb", 0, 0),
        ("zb", 0, 1), ("zb", 1, 0), ("zb", 1, 1), ("shift", 0), ("shift", 2), ("shift", 4), ("shift", 6),
        ("shift", 8), ("shift", 10), ("shift", 12), "kcms", "kcf", ("sm", 0, 0), ("sm", 0, 1),
        ("nm", 0, 0, 0), ("nm", 0, 0, 1), ("nm", 0, 1, 0), ("nm", 0, 1, 1), ("csm", 0), ("csm", 1), "cmax",
        "csub", "csum", "c01", "ccoef", "Pc", ("sm", 1, 0), ("sm", 1, 1), ("nm", 1, 0, 0), ("nm", 1, 0, 1),
        ("nm", 1, 1, 0), ("nm", 1, 1, 1), ("inv", 0), ("coef", 0), ("P", 0, 0, 0), ("P", 0, 0, 1),
        ("P", 0, 1, 0), ("P", 0), ("sm", 2, 0), ("sm", 2, 1), ("nm", 2, 0, 0), ("nm", 2, 0, 1),
        ("nm", 2, 1, 0), ("nm", 2, 1, 1), ("inv", 1), ("coef", 1), ("P", 1, 0, 0), ("P", 1, 0, 1),
        ("P", 1, 1, 0), ("P", 1), ("sm", 3, 0), ("sm", 3, 1), ("nm", 3, 0, 0), ("nm", 3, 0, 1),
        ("nm", 3, 1, 0), ("nm", 3, 1, 1), ("inv", 2), ("coef", 2), ("P", 2, 0, 0), ("P", 2, 0, 1),
        ("P", 2, 1, 0), ("P", 2), ("sm", 4, 0), ("sm", 4, 1), ("nm", 4, 0, 0), ("nm", 4, 0, 1),
        ("nm", 4, 1, 0), ("nm", 4, 1, 1), ("inv", 3), ("coef", 3), ("P", 3, 0, 0), ("P", 3, 0, 1),
        ("P", 3, 1, 0), ("P", 3), ("sm", 5, 0), ("sm", 5, 1), ("nm", 5, 0, 0), ("nm", 5, 0, 1),
        ("nm", 5, 1, 0), ("nm", 5, 1, 1), ("inv", 4), ("coef", 4), ("P", 4, 0, 0), ("P", 4, 0, 1),
        ("P", 4, 1, 0), ("P", 4), ("sm", 6, 0), ("sm", 6, 1), ("nm", 6, 0, 0), ("nm", 6, 0, 1),
        ("nm", 6, 1, 0), ("nm", 6, 1, 1), ("inv", 5), ("coef", 5), ("P", 5, 0, 0), ("P", 5, 0, 1),
        ("P", 5, 1, 0), ("P", 5), ("sm", 7, 0), ("sm", 7, 1), ("nm", 7, 0, 0), ("nm", 7, 0, 1),
        ("nm", 7, 1, 0), ("nm", 7, 1, 1), ("inv", 6), ("coef", 6), ("P", 6, 0, 0), ("P", 6, 0, 1),
        ("P", 6, 1, 0), ("P", 6), ("inv", 7), ("coef", 7), ("P", 7, 0, 0), ("P", 7, 0, 1), ("P", 7, 1, 0),
        ("P", 7), "lw", ("cs", 0), ("cs", 1), ("cs", 2), ("cs", 3), "csp", "kmx", "krnx", ("kkn", 0),
        ("kkn", 1), "bb", ("ka1", 0), ("ka1", 1), ("ka1", 2), ("ka1", 3), "kp", ("rk", 0), ("rk", 1),
        ("rk", 2), ("rk", 3), "cwl", ("bonus", 0), ("bonus", 1), ("G1", 0, 0), ("G1", 0, 1), ("RK", 0, 0),
        ("RK", 0, 1), ("RB", 0, 0), ("RB", 0, 1), ("gv", 0), ("kv", 0, 0), ("kv", 0, 1), ("N1", 0, 0),
        ("SA", 0, 0), ("M2", 0, 0), ("M", 0, 0), ("N1", 0, 1, 0), ("N1", 0, 1), ("SA", 0, 1), ("M1", 0, 1),
        ("M2", 0, 1), ("M", 0, 1), ("yb0", 0), ("yb", 0, 0), ("N1", 0, 2, 0), ("N1", 0, 2), ("SA", 0, 2),
        ("M1", 0, 2), ("M2", 0, 2), ("M", 0, 2), ("N1", 0, 3, 0), ("N1", 0, 3), ("SA", 0, 3), ("yb", 0, 1),
        ("G1", 1, 0), ("G1", 1, 1), ("RK", 1, 0), ("RK", 1, 1), ("RB", 1, 0), ("RB", 1, 1), ("gv", 1),
        ("kv", 1, 0), ("kv", 1, 1), ("N1", 1, 0), ("SA", 1, 0), ("M2", 1, 0), ("M", 1, 0), ("N1", 1, 1, 0),
        ("N1", 1, 1), ("SA", 1, 1), ("M1", 1, 1), ("M2", 1, 1), ("M", 1, 1), ("yb0", 1), ("yb", 1, 0),
        ("N1", 1, 2, 0), ("N1", 1, 2), ("SA", 1, 2), ("M1", 1, 2), ("M2", 1, 2), ("M", 1, 2),
        ("N1", 1, 3, 0), ("N1", 1, 3), ("SA", 1, 3), ("yb", 1, 1), "ysum", "ymean", "ycen", "ysqs", "yvar",
        "yn", "ybon",
    ],
    "pool": [
        "qrn", "fresh1", "cneg0", "cmask0", "cm01_0", "fresh", ("cneg", 0), ("cneg", 2), ("cm", -1e+30),
        ("cm", 0.0), "masks", "krn", ("v", 0, 0), ("v", 0, 1), ("v", 1, 0), "v", "kcrn", "cinv", "kkrn",
        "al", "rt", "be", "ka", "tmp_free", "yrn", "or", "on_low", "or_low", ("y", 0, 0), ("y", 0),
        ("y", 1, 0), ("y", 1),
    ],
}


def build(nc, ins, out, stages):
    groups = weight_groups(ins)
    groups = [g for g in groups if g[0].rsplit("_", 1)[0] in stages or g[0] in stages]
    tile_of = []
    tiles = []
    for gi, (_, _, cols, piece, k) in enumerate(groups):
        tile_of.append(len(tiles))
        for k0 in range(0, k, ROWS):
            tiles.append((gi, k0, min(ROWS, k - k0)))
    first = {}
    for gi, g in enumerate(groups):
        first.setdefault(g[0], gi)
    width = [len(g[2]) * g[3] for g in groups]

    ctx = ExitStack()
    with ctx:
        def sb(name, shape, dt=F32):
            return ctx.enter_context(nc.sbuf_tensor(name, shape, dt))

        def at(name, shape, off, dt=F32):
            return nc.alloc_sbuf_tensor_at(name, shape, dt, offset=off)

        def sem(name):
            return ctx.enter_context(nc.semaphore(name))

        raw = [sb(f"raw{i}", [P, ROWS * GW]) for i in range(RING)]
        high = [sb(f"high{i}", [P, ROWS * GW], F32R) for i in range(2)]
        low = [sb(f"low{i}", [P, ROWS * GW], F32R) for i in range(2)]
        xh = sb("xh", [P, DC, SEQ], F32R)
        xl = sb("xl", [P, DC, SEQ], F32R)
        slab_at = nc.sbuf_base
        slab = sb("slab", [P, 2 * FC * SEQ])
        hh = at("hh", [P, FC, SEQ], slab_at, F32R)
        hl = at("hl", [P, FC, SEQ], slab_at + FC * SEQ * 4, F32R)
        res = sb("res", [P, TB, D])
        work_at = nc.sbuf_base
        work = sb("work", [P, TB, D])
        gain_at = nc.sbuf_base
        gain = [sb(f"gain{i}", [P, D]) for i in range(2)]
        ident = sb("ident", [P, P])
        ones = sb("ones", [P, P])
        mhalf = sb("mhalf", [P, 32])
        minus1 = sb("minus1", [P, 48])
        upto = sb("upto", [P, P])
        beyond = sb("beyond", [P, P])
        lvmask = sb("lvmask", [P, 7, 64])
        gate_s = [[sb(f"gate_s{i}{t}", [P, 256]) for t in range(TB)] for i in range(2)]
        prod = [[sb(f"prod{i}{t}", [P, GW]) for t in range(TB)] for i in range(2)]
        ssq = sb("ssq", [P, TB, 2])
        msq = sb("msq", [P, TB])
        rstd = sb("rstd", [P, TB])
        pss = sb("pss", [P, TB])
        pms = sb("pms", [P, TB])
        prs = sb("prs", [P, TB])

        vec_rows = column_rows(ins)
        vec = sb("vec", [P, 5 * P])
        stage_rows = [work[:, b // 4, (b % 4) * P:(b % 4 + 1) * P] for b in range(5)]
        col = {}
        for b, part in enumerate(vec_rows):
            r = 0
            for name, _, n in part:
                col[name] = (b, r)
                r += n

        def vcol(name, i):
            b, r = col[name]
            at_ = b * P + r
            return vec[:, at_ + i:at_ + i + 1] if isinstance(i, int) else vec[:, bass.ds(i + at_, 1)]

        acc = [[ctx.enter_context(nc.psum_tensor(f"acc{i}{t}", [P, GW], F32)) for t in range(TB)] for i in range(2)]
        tr = [ctx.enter_context(nc.psum_tensor(f"tr{i}", [P, GW], F32)) for i in range(2)]
        aux = [ctx.enter_context(nc.psum_tensor(f"aux{i}", [P, GW], F32)) for i in range(2)]

        landed = [sem(f"landed{i}") for i in range(RING)]
        high_ready = sem("high_ready")
        low_ready = [sem("low_ready_even"), sem("low_ready_odd")]
        used = sem("used")
        acc_ready = sem("acc_ready")
        acc_free = [[sem(f"acc_free{i}{t}") for t in range(TB)] for i in range(2)]
        tr_ready = sem("tr_ready")
        tr_free = [sem(f"tr_free{i}") for i in range(2)]
        rows_in = sem("rows_in")
        res_in = sem("res_in")
        gain_in = [sem(f"gain_in{i}") for i in range(2)]
        ident_zero = sem("ident_zero")
        consts = sem("consts")
        vec_tr = sem("vec_tr")
        vec_ready = sem("vec_ready")
        pre_sq = sem("pre_sq")
        pre_ms = sem("pre_ms")
        pre_rstd = sem("pre_rstd")
        normed = sem("normed")
        xh_ready = sem("xh_ready")
        xl_ready = sem("xl_ready")
        post_sq = sem("post_sq")
        post_sum = sem("post_sum")
        post_ms = sem("post_ms")
        post_rstd = sem("post_rstd")
        res_ready = sem("res_ready")
        silu_ready = sem("silu_ready")
        hh_ready = sem("hh_ready")
        conv0 = sem("conv0")
        conv_tap1 = sem("conv_tap1")
        conv_half = sem("conv_half")
        sc_hh = sem("sc_hh")
        sc_hl = sem("sc_hl")
        stored = sem("stored")

        arena_at = nc.sbuf_base
        arena = sb("arena", [P, 10 * 1024])

        class Carve:
            def __init__(self, start, size):
                self.at, self.end = start, start + size

            def __call__(self, name, shape, dt=F32):
                t = at(name, [P] + shape, self.at, dt)
                self.at += 4 * int(np.prod(shape))
                assert self.at <= self.end, name
                return t
        conv_fm = arena[:, 0:DC * SEQ].rearrange("p (c t) -> p c t", c=DC)
        y_fm = [arena[:, (DC + 2 * i) * SEQ:(DC + 2 * i + 2) * SEQ] for i in range(2)]

        plan = dict(unit=0, pre=0, post=0, sil=0, hhc=0)


        early = [0]
        for t, (gi, k0, kn) in enumerate(tiles):
            early.append(early[-1] + (k0 + kn < groups[gi][4]))

        def wait_used(eng, t, i=0):
            gi, k0, kn = tiles[t]
            if k0 + kn == groups[gi][4]:
                eng.wait_ge(acc_ready, 2 * gi + 2 + 4 * i)
            else:
                eng.wait_ge(used, early[t + 1] + 2 * i)

        def load(sp, t, i=0, step=0):
            gi, k0, kn = tiles[t]
            n = width[gi]
            _, w, cols, piece, _ = groups[gi]
            if groups[gi][0].startswith("mix_pn"):
                sp.wait_ge(high_ready, t - RING + 1)
                sp.wait_ge(low_ready[t % 2], (t - RING) // 2 + 1)
                dst = raw[t % RING][:, 0:kn * n].rearrange("p (k n) -> p k n", k=kn)
                for h in range(2):
                    src = w[h * 256:(h + 1) * 256, cols[0]:cols[0] + n].rearrange("(k p) c -> p k c", p=64)
                    sp.dma_start(dst[h * 64:(h + 1) * 64], src).then_inc(landed[t % RING], 16)
                return
            if t >= RING or not isinstance(i, int):
                highs, lows = t - RING + 1 + 4 * i, (t - RING) // 2 + 1 + 2 * i
                if not isinstance(i, int):
                    highs, lows = sp.to_reg(highs), sp.to_reg(lows)
                sp.wait_ge(high_ready, highs)
                sp.wait_ge(low_ready[t % 2], lows)
                if not isinstance(i, int):
                    sp.nop(nofuse=True)
            rows = w.rearrange("(k p) c -> p k c", p=P)[:, k0:k0 + kn, :]
            dst = raw[t % RING][:, 0:kn * n].rearrange("p (k n) -> p k n", k=kn)
            for h in range(2):
                if len(cols) == 2:
                    at_ = cols[h]
                    c = slice(at_, at_ + piece) if isinstance(i, int) else bass.ds(i * step + at_, piece)
                    sp.dma_start(dst[:, :, h * piece:(h + 1) * piece], rows[:, :, c]).then_inc(landed[t % RING], 16)
                else:
                    ks = slice(h * kn // 2, (h + 1) * kn // 2)
                    sp.dma_start(dst[:, ks, :], rows[:, ks, cols[0]:cols[0] + n]).then_inc(landed[t % RING], 16)

        def split_high(act, t, i=0):
            if t >= len(tiles):
                return
            gi, k0, kn = tiles[t]
            n = kn * width[gi]
            act.wait_ge(landed[t % RING], 32 * (t // RING + 1) + 32 * i)
            if t >= 2:
                wait_used(act, t - 2, i)
            nc.scalar.activation(high[t % 2][:, 0:n], raw[t % RING][:, 0:n], ACT.Copy).then_inc(high_ready, 1)

        def split_low(eng, t, i=0):
            if t >= len(tiles):
                return
            gi, k0, kn = tiles[t]
            n = kn * width[gi]
            eng.wait_ge(high_ready, t + 1 + 4 * i)
            nc.vector.tensor_tensor(low[t % 2][:, 0:n], raw[t % RING][:, 0:n],
                            high[t % 2][:, 0:n].bitcast(F32), ALU.subtract).then_inc(low_ready[t % 2], 1)

        def group_tiles(gi):
            return range(tile_of[gi], tile_of[gi] + (groups[gi][4] + ROWS - 1) // ROWS)

        def stream_act(act, gi, i=0):
            for t in group_tiles(gi):
                split_high(act, t + 2, i)

        def stream_dve(dve, gi, i=0):
            for t in group_tiles(gi):
                split_low(dve, t + 2, i)

        def products(pe, gi, xa, xb, i=0, before=None):
            n = width[gi]
            k = groups[gi][4]
            for t in group_tiles(gi):
                _, k0, kn = tiles[t]
                pe.wait_ge(low_ready[t % 2], t // 2 + 1 + 2 * i)
                if before is not None:
                    before(k0, kn)
                last = k0 + kn == k
                for tb in range(TB):
                    if k0 == 0 and (gi >= 2 or not isinstance(i, int)):
                        pe.wait_ge(acc_free[gi % 2][tb], gi // 2 + i)
                    o = acc[gi % 2][tb][:, 0:n]
                    for kk in range(kn):
                        wh = high[t % 2][:, kk * n:(kk + 1) * n]
                        wl = low[t % 2][:, kk * n:(kk + 1) * n]
                        a = xa[:, k0 + kk, tb * P:(tb + 1) * P]
                        b = xb[:, k0 + kk, tb * P:(tb + 1) * P]
                        nc.tensor.matmul(o, a, wh, start=(k0 + kk == 0), stop=False)
                        nc.tensor.matmul(o, a, wl, start=False, stop=False)
                        mm = nc.tensor.matmul(o, b, wh, start=False, stop=(k0 + kk == k - 1))
                    if last:
                        mm.then_inc(acc_ready, 1)
                if not last:
                    mm.then_inc(used, 1)

        def free_unit(pe, u, i=0):
            if u >= 2:
                pe.wait_ge(tr_free[u % 2], u // 2 + i)

        def prenorm_act(act, n, unit, g0):
            for tb in range(TB):
                if n == 0:
                    act.wait_ge(res_in, 16)
                    act.wait_ge(vec_ready, 5)
                else:
                    act.wait_ge(res_ready, 4 * (n - 1) + 2 * tb + 2)
                nc.scalar.activation(work[:, tb, :], res[:, tb, :], ACT.Square,
                                     accum_out=pss[:, tb:tb + 1]).then_inc(pre_sq, 1)
            for c in range(DC):
                if c % 2 == 0:
                    act.wait_ge(tr_ready, unit + c // 2 + 1)
                src = tr[(unit + c // 2) % 2][:, (c % 2) * SEQ:(c % 2 + 1) * SEQ]
                nc.scalar.activation(xh[:, c, :], src, ACT.Copy, scale=g0(c)).then_inc(xh_ready, 1)

        def prenorm_dve(dve, n, unit, g0):
            for tb in range(TB):
                dve.wait_ge(pre_sq, TB * n + tb + 1)
                nc.vector.tensor_scalar(pms[:, tb:tb + 1], pss[:, tb:tb + 1], 1.0 / D, EPS,
                                        ALU.mult, ALU.add).then_inc(pre_ms, 1)
            for tb in range(TB):
                dve.wait_ge(pre_rstd, TB * n + tb + 1)
                nc.vector.tensor_scalar(work[:, tb, :], res[:, tb, :], prs[:, tb:tb + 1], None,
                                        ALU.mult).then_inc(normed, 1)
            for c in range(DC):
                u = unit + c // 2
                dve.wait_ge(xh_ready, DC * n + c // 2 * 2 + 2)
                ins_ = nc.vector.scalar_tensor_tensor(xl[:, c, :], tr[u % 2][:, (c % 2) * SEQ:(c % 2 + 1) * SEQ],
                                                      g0(c), xh[:, c, :].bitcast(F32), ALU.mult, ALU.subtract)
                ins_.then_inc(xl_ready if c % 2 == 0 else tr_free[u % 2], 1)

        def prenorm_pool(pool, n):
            for tb in range(TB):
                pool.wait_ge(pre_ms, TB * n + tb + 1)
                nc.gpsimd.tensor_tensor(prs[:, tb:tb + 1], pms[:, tb:tb + 1], mhalf[:, 0:1],
                                        ALU.pow).then_inc(pre_rstd, 1)

        def keep_clock(pe, count, bank=aux[1]):
            for _ in range(count):
                nc.tensor.matmul(bank[:, 0:P], ident[:, :], ones[:, :], start=True, stop=True)

        def prenorm_pe(pe, n, unit):
            pe.wait_ge(vec_ready, 5)
            pe.wait_ge(pre_sq, TB * n + 1)
            keep_clock(pe, 9)
            pe.wait_ge(normed, TB * (n + 1))
            for u in range(unit, unit + DC // 2):
                free_unit(pe, u)
                for c in range(2):
                    for tb in range(TB):
                        ch = 2 * (u - unit) + c
                        mm = nc.tensor.transpose(tr[u % 2][:, c * SEQ + tb * P:c * SEQ + (tb + 1) * P],
                                                 work[:, tb, ch * P:(ch + 1) * P], ident[:, :])
                mm.then_inc(tr_ready, 1)

        def wait_x(pe, unit):
            def before(k0, kn):
                u = unit + (k0 + kn) // 2 - 1
                for v in (u - 1, u):
                    pe.wait_ge(tr_free[v % 2], v // 2 + 1)
            return before

        def postnorm_act(act, n, gi):
            for c in range(2):
                for tb in range(TB):
                    act.wait_ge(acc_ready, 2 * (gi + c) + tb + 1)
                    nc.scalar.activation(work[:, tb, c * GW:(c + 1) * GW], acc[(gi + c) % 2][tb][:, :], ACT.Square,
                                         accum_out=ssq[:, tb, c:c + 1]).then_inc(post_sq, 1)
                if c == 0:
                    for t in group_tiles(gi + 1)[:-1]:
                        split_high(act, t + 2)
            split_high(act, group_tiles(gi + 1)[-1] + 2)

        def add_branch(dve, gi, tb):
            for c in range(2):
                dve.wait_ge(acc_free[(gi + c) % 2][tb], (gi + c) // 2 + 1)
                h = res[:, tb, c * GW:(c + 1) * GW]
                nc.vector.tensor_tensor(h, h, work[:, tb, c * GW:(c + 1) * GW], ALU.add).then_inc(res_ready, 1)

        def postnorm_dve(dve, n, gi, factor):
            stream_dve(dve, gi)
            for t in group_tiles(gi + 1)[:-1]:
                split_low(dve, t + 2)
            dve.wait_ge(post_sq, 4 * (n + 1))
            nc.vector.tensor_tensor(msq[:, :], ssq[:, :, 0], ssq[:, :, 1], ALU.add).then_inc(post_sum, 1)
            dve.wait_ge(post_sum, n + 1)
            f = 1.0 / factor ** 2
            nc.vector.tensor_scalar(msq[:, :], msq[:, :], f / D, EPS * f, ALU.mult, ALU.add).then_inc(post_ms, 1)
            dve.wait_ge(post_rstd, n + 1)
            dve.wait_ge(gain_in[n % 2], 16 * (n // 2 + 1))
            for tb in range(TB):
                for c in range(2):
                    nc.vector.scalar_tensor_tensor(
                        work[:, tb, c * GW:(c + 1) * GW], acc[(gi + c) % 2][tb][:, :], rstd[:, tb:tb + 1],
                        gain[n % 2][:, c * GW:(c + 1) * GW], ALU.mult, ALU.mult,
                    ).then_inc(acc_free[(gi + c) % 2][tb], 1)
                add_branch(dve, gi, tb)
            split_low(dve, group_tiles(gi + 1)[-1] + 2)

        def postnorm_pool(pool, n, gi):
            pool.wait_ge(post_ms, n + 1)
            nc.gpsimd.tensor_tensor(rstd[:, :], msq[:, :], mhalf[:, 0:TB], ALU.pow).then_inc(post_rstd, 1)

        def gain_sp(sp, n, vector):
            if n >= 2:
                sp.wait_ge(res_ready, 4 * (n - 1))
            sp.dma_start(gain[n % 2][:, :], vector.partition_broadcast(P)).then_inc(gain_in[n % 2], 16)

        def silu(act, gi, sil, i=0):
            for tb in range(TB):
                act.wait_ge(acc_ready, 2 * gi + tb + 1 + 4 * i)
                nc.scalar.activation(gate_s[gi % 2][tb][:, :], acc[gi % 2][tb][:, 0:256], ACT.Silu).then_inc(silu_ready, 1)

        def gate_times_up(dve, gi, sil, i=0):
            for tb in range(TB):
                dve.wait_ge(silu_ready, sil + tb + 1 + 4 * i)
                nc.vector.tensor_tensor(prod[gi % 2][tb][:, 0:256], gate_s[gi % 2][tb][:, :], acc[gi % 2][tb][:, 256:512],
                                        ALU.mult).then_inc(acc_free[gi % 2][tb], 1)

        def transpose_prod(pe, gi, u, i=0):
            free_unit(pe, u, i)
            for tb in range(TB):
                pe.wait_ge(acc_free[gi % 2][tb], gi // 2 + 1 + i)
            for c in range(2):
                for tb in range(TB):
                    mm = nc.tensor.transpose(tr[u % 2][:, c * SEQ + tb * P:c * SEQ + (tb + 1) * P],
                                             prod[gi % 2][tb][:, c * P:(c + 1) * P], ident[:, :])
            mm.then_inc(tr_ready, 1)

        def hidden_high(act, g, u, i=0):
            act.wait_ge(tr_ready, u + 1 + 2 * i)
            flat = hh[:, :, :].rearrange("p c t -> p (c t)")
            dst = flat[:, g * 512:(g + 1) * 512] if isinstance(i, int) else flat[:, bass.ds(i * 1024 + g * 512, 512)]
            nc.scalar.activation(dst, tr[u % 2][:, :], ACT.Copy).then_inc(hh_ready, 1)

        def hidden_low(dve, g, u, hhc, i=0):
            dve.wait_ge(hh_ready, hhc + g + 1 + 2 * i)
            fh, fl = (x[:, :, :].rearrange("p c t -> p (c t)") for x in (hh, hl))
            s = slice(g * 512, (g + 1) * 512) if isinstance(i, int) else bass.ds(i * 1024 + g * 512, 512)
            nc.vector.tensor_tensor(fl[:, s], tr[u % 2][:, :], fh[:, s].bitcast(F32), ALU.subtract).then_inc(tr_free[u % 2], 1)

        FG = FC // 2
        LOOPS = (FG - 1) // 2

        class Ffn:
            def __init__(self, name, g0, vector):
                self.name, self.g0, self.gain = name, g0, vector
                self.up, self.down = first[name + "_up"], first[name + "_down"]
                self.n, self.post, self.sil, self.hhc = plan["pre"], plan["post"], plan["sil"], plan["hhc"]
                self.norm_unit = plan["unit"]
                self.unit = plan["unit"] + DC // 2
                plan["pre"] += 1
                plan["post"] += 1
                plan["unit"] += DC // 2 + FG
                plan["sil"] += 2 * FG
                plan["hhc"] += FG

            def sp(self, sp):
                gain_sp(sp, self.post, self.gain)
                for t in group_tiles(self.up):
                    load(sp, t)
                t0 = tile_of[self.up + 1]
                for t in range(t0, t0 + 4):
                    load(sp, t)
                with sp.Fori(1, LOOPS) as i:
                    for t in range(t0, t0 + 4):
                        load(sp, t, i, 512)
                for gi in (self.down, self.down + 1):
                    for t in group_tiles(gi):
                        load(sp, t)

            def pe(self, pe):
                prenorm_pe(pe, self.n, self.norm_unit)
                products(pe, self.up, xh, xl, before=wait_x(pe, self.norm_unit))
                with pe.Fori(0, LOOPS) as i:
                    for g in range(2):
                        products(pe, self.up + 1 + g, xh, xl, i)
                        transpose_prod(pe, self.up + g, self.unit + g, i)
                transpose_prod(pe, self.up + FG - 1, self.unit + FG - 1)

                def split(k0, kn):
                    for c in range(k0, k0 + kn, 2):
                        u = self.unit + c // 2
                        pe.wait_ge(tr_free[u % 2], u // 2 + 1)
                products(pe, self.down, hh, hl, before=split)
                products(pe, self.down + 1, hh, hl)

            def act(self, act):
                prenorm_act(act, self.n, self.norm_unit, self.g0)
                stream_act(act, self.up)
                silu(act, self.up, self.sil)
                with act.Fori(0, LOOPS) as i:
                    for g in range(2):
                        stream_act(act, self.up + 1 + g, i)
                        silu(act, self.up + 1 + g, self.sil + 2 + 2 * g, i)
                        hidden_high(act, g, self.unit + g, i)
                hidden_high(act, FG - 1, self.unit + FG - 1)
                stream_act(act, self.down)
                postnorm_act(act, self.post, self.down)

            def dve(self, dve):
                prenorm_dve(dve, self.n, self.norm_unit, self.g0)
                stream_dve(dve, self.up)
                gate_times_up(dve, self.up, self.sil)
                with dve.Fori(0, LOOPS) as i:
                    for g in range(2):
                        stream_dve(dve, self.up + 1 + g, i)
                        gate_times_up(dve, self.up + 1 + g, self.sil + 2 + 2 * g, i)
                        hidden_low(dve, g, self.unit + g, self.hhc, i)
                hidden_low(dve, FG - 1, self.unit + FG - 1, self.hhc)
                postnorm_dve(dve, self.post, self.down, 0.5)

            def pool(self, pool):
                prenorm_pool(pool, self.n)
                postnorm_pool(pool, self.post, self.down)

        class ShortConv:
            def __init__(self):
                self.cv, self.b, self.out = first["sc_cv"], first["sc_b"], first["sc_out"]
                self.n, self.post = plan["pre"], plan["post"]
                self.norm_unit = plan["unit"]
                self.unit = plan["unit"] + DC // 2
                plan["pre"] += 1
                plan["post"] += 1
                self.sil = plan["sil"]
                plan["sil"] += 8
                plan["unit"] += DC // 2 + 4 + 4
                self.g0 = lambda c: vcol("norm_g", 2 * DC + c)

            def sp(self, sp):
                gain_sp(sp, self.post, ins["norm_g"][0, 3, :])
                for gi in range(self.cv, self.out + 2):
                    for t in group_tiles(gi):
                        load(sp, t)

            def pe(self, pe):
                prenorm_pe(pe, self.n, self.norm_unit)
                products(pe, self.cv, xh, xl, before=wait_x(pe, self.norm_unit))
                for g in range(1, 4):
                    products(pe, self.cv + g, xh, xl)
                    transpose_prod(pe, self.cv + g - 1, self.unit + g - 1)
                products(pe, self.b, xh, xl)
                transpose_prod(pe, self.cv + 3, self.unit + 3)
                products(pe, self.b + 1, xh, xl)
                for g in range(2):
                    for h in range(2):
                        u = self.unit + 4 + 2 * g + h
                        free_unit(pe, u)
                        for tb in range(TB):
                            pe.wait_ge(acc_free[(self.b + g) % 2][tb], (self.b + g) // 2 + 1)
                        for c in range(2):
                            for tb in range(TB):
                                mm = nc.tensor.transpose(
                                    tr[u % 2][:, c * SEQ + tb * P:c * SEQ + (tb + 1) * P],
                                    prod[(self.b + g) % 2][tb][:, (2 * h + c) * P:(2 * h + c + 1) * P], ident[:, :])
                        mm.then_inc(tr_ready, 1)

                def split(k0, kn):
                    pe.wait_ge(sc_hl, (k0 + kn) // 2)
                products(pe, self.out, hh, hl, before=split)
                products(pe, self.out + 1, hh, hl)

            def conv_act(self, act, g):
                u = self.unit + g
                act.wait_ge(tr_ready, u + 1)
                for c in range(2):
                    nc.scalar.activation(conv_fm[:, 2 * g + c, :], tr[u % 2][:, c * SEQ:(c + 1) * SEQ], ACT.Copy,
                                         scale=vcol("sc_conv", 2 * DC + 2 * g + c)).then_inc(conv0, 1)

            def act(self, act):
                prenorm_act(act, self.n, self.norm_unit, self.g0)
                for g in range(4):
                    stream_act(act, self.cv + g)
                    for tb in range(TB):
                        act.wait_ge(acc_ready, 2 * (self.cv + g) + tb + 1)
                        nc.scalar.activation(gate_s[(self.cv + g) % 2][tb][:, :], acc[(self.cv + g) % 2][tb][:, 0:256],
                                             ACT.Copy).then_inc(silu_ready, 1)
                    if g:
                        self.conv_act(act, g - 1)
                for g in range(2):
                    gi = self.b + g
                    stream_act(act, gi)
                    for tb in range(TB):
                        act.wait_ge(acc_ready, 2 * gi + tb + 1)
                        nc.scalar.activation(prod[gi % 2][tb][:, :], acc[gi % 2][tb][:, :],
                                             ACT.Copy).then_inc(acc_free[gi % 2][tb], 1)
                    if g == 0:
                        self.conv_act(act, 3)
                for u in range(4):
                    v = self.unit + 4 + u
                    act.wait_ge(tr_free[v % 2], v // 2 + 1)
                    nc.scalar.activation(hh[:, 2 * u:2 * u + 2, :].rearrange("p c t -> p (c t)"), y_fm[u % 2],
                                         ACT.Copy).then_inc(sc_hh, 1)
                stream_act(act, self.out)
                postnorm_act(act, self.post, self.out)

            def conv_dve(self, dve, g):
                u = self.unit + g
                for c in range(2):
                    ch = 2 * g + c
                    src = tr[u % 2][:, c * SEQ:(c + 1) * SEQ]
                    dve.wait_ge(conv0, 2 * g + 2)
                    nc.vector.scalar_tensor_tensor(
                        conv_fm[:, ch, 1:], src[:, 0:SEQ - 1], vcol("sc_conv", DC + ch), conv_fm[:, ch, 1:],
                        ALU.mult, ALU.add).then_inc(conv_tap1, 1)
                    dve.wait_ge(conv_tap1, ch + 1)
                    nc.vector.scalar_tensor_tensor(
                        conv_fm[:, ch, 2:], src[:, 0:SEQ - 2], vcol("sc_conv", ch), conv_fm[:, ch, 2:],
                        ALU.mult, ALU.add).then_inc(conv_half if c == 0 else tr_free[u % 2], 1)

            def dve(self, dve):
                prenorm_dve(dve, self.n, self.norm_unit, self.g0)
                for g in range(4):
                    stream_dve(dve, self.cv + g)
                    gate_times_up(dve, self.cv + g, self.sil + 2 * g)
                    if g:
                        self.conv_dve(dve, g - 1)
                stream_dve(dve, self.b)
                self.conv_dve(dve, 3)
                stream_dve(dve, self.b + 1)
                v = self.unit + 3
                dve.wait_ge(tr_free[v % 2], v // 2 + 1)
                for u in range(4):
                    v = self.unit + 4 + u
                    dve.wait_ge(tr_ready, v + 1)
                    if u >= 2:
                        dve.wait_ge(sc_hl, u - 1)
                    nc.vector.tensor_tensor(y_fm[u % 2], tr[v % 2][:, :],
                                            conv_fm[:, 2 * u:2 * u + 2, :].rearrange("p c t -> p (c t)"),
                                            ALU.mult).then_inc(tr_free[v % 2], 1)
                postnorm_dve(dve, self.post, self.out, 1.0)

            def pool(self, pool):
                prenorm_pool(pool, self.n)
                for u in range(4):
                    pool.wait_ge(sc_hh, u + 1)
                    nc.gpsimd.tensor_tensor(hl[:, 2 * u:2 * u + 2, :].rearrange("p c t -> p (c t)"), y_fm[u % 2],
                                            hh[:, 2 * u:2 * u + 2, :].rearrange("p c t -> p (c t)").bitcast(F32),
                                            ALU.subtract).then_inc(sc_hl, 1)
                postnorm_pool(pool, self.post, self.out)

        def g1(i, n):
            return lambda c: vcol("norm_g", (6 * i + n) * DC + c)


        class Inverse:
            def __init__(self, tag, n, levels, A, U, T, X):
                self.n, self.levels, self.A, self.U, self.T, self.X = n, levels, A, U, T, X
                self.h = n // 2
                self.bx, self.bu, self.bt = acc[0], acc[1], (aux[0], tr[0])
                self.identity = sem(tag + "_identity")
                self.x_psum = sem(tag + "_x_psum")
                self.x_ready = sem(tag + "_x_ready")
                self.u_psum = sem(tag + "_u_psum")
                self.t_psum = sem(tag + "_t_psum")
                self.u_ready = sem(tag + "_u_ready")
                self.t_ready = sem(tag + "_t_ready")

            def second(self, m, l):
                return m.rearrange("p j (k two b) -> p j k two b", two=2, b=1 << l)[:, :, :, 1, :]

            def half(self, h):
                return range(h * self.h, (h + 1) * self.h)

            def pool(self, pool, r):
                if r and self.used is not None:
                    pool.wait_ge(self.used, r)
                nc.gpsimd.tensor_copy(self.U[:, :, :], ident[:, :].unsqueeze(1).broadcast_to([P, self.n, P])).then_inc(self.identity, 1)

            def turn(self, m, h):
                for j in self.half(h):
                    mm = nc.tensor.transpose(self.bt[h][:, (j % self.h) * P:(j % self.h + 1) * P], m[:, j, :], ident[:, :])
                return mm

            def pe(self, pe, r):
                L, n = self.levels, self.n
                for h in range(2):
                    self.turn(self.A, h).then_inc(self.x_psum, 1)
                keep_clock(pe, 4)
                for l in range(1, L):
                    for h in range(2):
                        pe.wait_ge(self.u_ready, 2 * (r * L + l - 1) + h + 1)
                        self.turn(self.U, h).then_inc(self.t_psum, 1)
                        for j in self.half(h):
                            c = (j % self.h) * 64
                            mm = nc.tensor.matmul(self.bx[h][:, c:c + 64], self.A[:, j, :], self.second(self.U[:, :, :], l)[:, j], start=True, stop=True)
                        mm.then_inc(self.x_psum, 1)
                    for h in range(2):
                        pe.wait_ge(self.x_ready, 2 * (r * L + l) + h + 1)
                        pe.wait_ge(self.t_ready, 2 * (r * (L - 1) + l - 1) + h + 1)
                        for j in self.half(h):
                            c = (j % self.h) * 64
                            mm = nc.tensor.matmul(self.bu[h][:, c:c + 64], self.T[:, j, :], self.X[:, j, :], start=True, stop=True)
                        mm.then_inc(self.u_psum, 1)

            def act(self, act, r):
                for l in range(self.levels - 1):
                    for h in range(2):
                        k = 2 * (r * (self.levels - 1) + l) + h + 1
                        act.wait_ge(self.t_psum, k)
                        nc.scalar.activation(self.T[:, h * self.h:(h + 1) * self.h, :].rearrange("p j c -> p (j c)"), self.bt[h][:, :],
                                             ACT.Copy).then_inc(self.t_ready, 1)

            def dve(self, dve, r):
                L, n = self.levels, self.h
                for l in range(L):
                    b = 1 << l
                    mask = lvmask[:, l, :].rearrange("p (k b) -> p k b", b=b).unsqueeze(1).broadcast_to([P, n, 64 // b, b])
                    blocks = [x.rearrange("p j (k b) -> p j k b", b=b) for x in (self.X[:, 0:n, :], self.X[:, n:2 * n, :])]
                    for h in range(2):
                        dve.wait_ge(self.x_psum, 2 * (r * L + l) + h + 1)
                        if l:
                            x = self.bx[h][:, 0:n * 64].rearrange("p (j k b) -> p j k b", j=n, b=b)
                        else:
                            x = self.second(self.bt[h][:, :].rearrange("p (j c) -> p j c", j=n), 0)
                        nc.vector.tensor_tensor(blocks[h], x, mask, ALU.mult).then_inc(self.x_ready, 1)
                    for h in range(2):
                        u = self.second(self.U[:, h * n:(h + 1) * n, :], l)
                        if l:
                            dve.wait_ge(self.u_psum, 2 * (r * (L - 1) + l - 1) + h + 1)
                            d = self.bu[h][:, 0:n * 64].rearrange("p (j k b) -> p j k b", j=n, b=b)
                        else:
                            dve.wait_ge(self.x_ready, 2 * r * L + h + 1)
                            dve.wait_ge(self.identity, r + 1)
                            d = blocks[h]
                        nc.vector.tensor_tensor(u, u, d, ALU.subtract).then_inc(self.u_ready, 1)

        class GatedDelta:
            NB = KH // 2

            def __init__(self):
                self.ba, self.qkv, self.z, self.out = (first["gdn_" + x] for x in ("ba", "qkv", "z", "out"))
                self.n, self.post = plan["pre"], plan["post"]
                self.norm_unit = plan["unit"]
                self.unit = plan["unit"] + DC // 2
                self.zunit = self.unit + 16
                plan["pre"] += 1
                plan["post"] += 1
                plan["unit"] += DC // 2 + 16 + 8
                self.g0 = g1(1, 2)
                c = Carve(arena_at, 10 * 4096)
                self.qf = c("gdn_qf", [KH, SEQ])
                self.kf = c("gdn_kf", [KH, SEQ])
                self.kt = c("gdn_kt", [TB, KH, P])
                self.vb = c("gdn_vb", [TB, VH, P])
                c = Carve(slab_at, 2 * FC * SEQ * 4)
                self.gm = c("gdn_gm", [8, P])
                self.A = c("gdn_A", [8, P])
                self.qk = c("gdn_qk", [8, P])
                self.U = c("gdn_U", [8, P])
                self.T = c("gdn_T", [8, P])
                self.X = c("gdn_X", [8, 64])
                self.vn = c("gdn_vn", [TB, 4, P])
                self.vt = c("gdn_vt", [4, P])
                self.S = c("gdn_S", [4, P])
                self.qS = c("gdn_qS", [4, P])
                c = Carve(slab_at, 2 * FC * SEQ * 4)
                self.cv = [c(f"gdn_cv{i}", [512]) for i in range(2)]
                self.sq = c("gdn_sq", [512])
                self.qt = c("gdn_qt", [512])
                self.osq = c("gdn_osq", [TB, VH, P])
                c = Carve(slab_at + (FC + 2 * DC) * SEQ * 4, (FC - 2 * DC) * SEQ * 4)
                self.s_e = c("gdn_e", [TB, 48])
                self.s_beta = c("gdn_beta", [TB, VH])
                self.s_x = c("gdn_x", [TB, VH])
                self.s_g = c("gdn_g", [TB, VH])
                self.s_alog = c("gdn_alog", [VH])
                self.s_dtb = c("gdn_dtb", [VH])
                self.s_eg = c("gdn_eg", [VH])
                self.s_etail = c("gdn_etail", [VH])
                self.s_nbe = c("gdn_nbe", [VH])
                self.ss, self.rn = c("gdn_ss", [8]), c("gdn_rn", [8])
                self.ss, self.rn = self.ss[:, 0:4], self.rn[:, 0:4]
                self.oss, self.orn = c("gdn_oss", [TB, VH]), c("gdn_orn", [TB, VH])
                self.g_small_in = sem("gdn_small_in")
                self.g_e1 = sem("gdn_e1")
                self.g_ax = sem("gdn_ax")
                self.g_axn = sem("gdn_axn")
                self.g_absx = sem("gdn_absx")
                self.g_e2 = sem("gdn_e2")
                self.g_ln = sem("gdn_ln")
                self.g_beta1 = sem("gdn_beta1")
                self.g_beta_ready = sem("gdn_beta_ready")
                self.g_ea = sem("gdn_ea")
                self.g_g_ready = sem("gdn_g_ready")
                self.g_sp = sem("gdn_sp")
                self.g_G_psum = sem("gdn_G_psum")
                self.g_eg_ready = sem("gdn_eg_ready")
                self.g_nbe_ready = sem("gdn_nbe_ready")
                self.g_tap3 = sem("gdn_tap3")
                self.g_taps = sem("gdn_taps")
                self.g_silu = sem("gdn_silu")
                self.g_t2 = sem("gdn_t2")
                self.g_t2sq = sem("gdn_t2sq")
                self.g_t2red = sem("gdn_t2red")
                self.g_t2ms = sem("gdn_t2ms")
                self.g_t2rn = sem("gdn_t2rn")
                self.g_t2out = sem("gdn_t2out")
                self.g_t3 = sem("gdn_t3")
                self.g_t3out = sem("gdn_t3out")
                self.g_kk = sem("gdn_kk")
                self.g_gm_ready = sem("gdn_gm_ready")
                self.g_D_psum = sem("gdn_D_psum")
                self.g_D_ready = sem("gdn_D_ready")
                self.g_A_ready = sem("gdn_A_ready")
                self.g_DT_ready = sem("gdn_DT_ready")
                self.g_qk_ready = sem("gdn_qk_ready")
                self.g_DT_masked = sem("gdn_DT_masked")
                self.g_v0_psum = sem("gdn_v0_psum")
                self.g_v0_ready = sem("gdn_v0_ready")
                self.g_vt_ready = sem("gdn_vt_ready")
                self.g_S_psum = sem("gdn_S_psum")
                self.g_S_ready = sem("gdn_S_ready")
                self.g_kS_psum = sem("gdn_kS_psum")
                self.g_qS_ready = sem("gdn_qS_ready")
                self.g_r_ready = sem("gdn_r_ready")
                self.g_v1_psum = sem("gdn_v1_psum")
                self.g_v1_ready = sem("gdn_v1_ready")
                self.g_o_psum = sem("gdn_o_psum")
                self.g_o_half = sem("gdn_o_half")
                self.g_o_ready = sem("gdn_o_ready")
                self.g_osq_ready = sem("gdn_osq_ready")
                self.g_ored = sem("gdn_ored")
                self.g_oms = sem("gdn_oms")
                self.g_orn_ready = sem("gdn_orn_ready")
                self.g_o_normed = sem("gdn_o_normed")
                self.g_o_gated = sem("gdn_o_gated")
                self.g_zsilu = sem("gdn_zsilu")
                self.g_zhh = sem("gdn_zhh")
                self.inv = Inverse("gdn_inv", 8, 7, self.A, self.U, self.T, self.X)
                self.inv.used = self.g_v1_psum

            def sp(self, sp):
                gain_sp(sp, self.post, ins["norm_g"][1, 3, :])
                for gi in range(self.ba, self.out + 2):
                    if gi == self.ba + 2:
                        if self.post:
                            sp.wait_ge(res_ready, 4 * self.post)
                        sp.dma_start(self.s_alog[:, :], ins["gdn_a_log"][0].partition_broadcast(P)).then_inc(self.g_small_in, 16)
                        sp.dma_start(self.s_dtb[:, :], ins["gdn_dt_bias"][0].partition_broadcast(P)).then_inc(self.g_small_in, 16)
                    for t in group_tiles(gi):
                        load(sp, t)

            def gates_act(self, act):
                gi = self.ba
                for tb in range(TB):
                    act.wait_ge(acc_ready, 2 * gi + tb + 1)
                    nc.scalar.activation(self.s_e[:, tb, 0:VH], acc[gi % 2][tb][:, 0:VH], ACT.Exp, scale=-1.0).then_inc(self.g_e1, 1)
                act.wait_ge(self.g_small_in, 32)
                nc.scalar.activation(self.s_alog[:, :], self.s_alog[:, :], ACT.Exp).then_inc(self.g_ea, 1)
                act.wait_ge(self.g_absx, 1)
                nc.scalar.activation(self.s_e[:, :, VH:2 * VH], self.s_e[:, :, 2 * VH:3 * VH], ACT.Exp, scale=-1.0).then_inc(self.g_e2, 1)
                act.wait_ge(self.g_e2, 1)
                nc.scalar.activation(self.s_e[:, :, VH:2 * VH], self.s_e[:, :, VH:2 * VH], ACT.Ln, bias=1.0).then_inc(self.g_ln, 1)
                act.wait_ge(self.g_G_psum, 1)
                nc.scalar.activation(self.s_eg[:, :], aux[1][:, 0:VH], ACT.Exp).then_inc(self.g_eg_ready, 1)
                nc.scalar.activation(self.s_etail[:, :], aux[1][:, VH:2 * VH], ACT.Exp).then_inc(self.g_eg_ready, 1)

            def gates_dve(self, dve):
                gi = self.ba
                dve.wait_ge(self.g_small_in, 32)
                for tb in range(TB):
                    dve.wait_ge(self.g_e1, tb + 1)
                    nc.vector.tensor_tensor(self.s_x[:, tb, :], acc[gi % 2][tb][:, VH:2 * VH], self.s_dtb[:, :],
                                            ALU.add).then_inc(acc_free[gi % 2][tb], 1)
                for tb in range(TB):
                    dve.wait_ge(acc_free[gi % 2][tb], gi // 2 + 1)
                nc.vector.tensor_scalar(self.s_e[:, :, 2 * VH:3 * VH], self.s_x[:, :, :], -1.0, None, ALU.mult).then_inc(self.g_axn, 1)
                dve.wait_ge(self.g_axn, 1)
                nc.vector.tensor_tensor(self.s_e[:, :, 2 * VH:3 * VH], self.s_e[:, :, 2 * VH:3 * VH], self.s_x[:, :, :],
                                        ALU.max).then_inc(self.g_absx, 1)
                dve.wait_ge(self.g_e1, TB)
                nc.vector.tensor_scalar(self.s_beta[:, :, :], self.s_e[:, :, 0:VH], 1.0, None, ALU.add).then_inc(self.g_beta1, 1)
                dve.wait_ge(self.g_ln, 1)
                nc.vector.scalar_tensor_tensor(self.s_x[:, :, :], self.s_x[:, :, :], 0.0, self.s_e[:, :, VH:2 * VH],
                                               ALU.max, ALU.add).then_inc(self.g_sp, 1)
                dve.wait_ge(self.g_sp, 1)
                dve.wait_ge(self.g_ea, 1)
                nc.vector.scalar_tensor_tensor(self.s_g[:, :, :], self.s_x[:, :, :], -1.0,
                                               self.s_alog[:, :].unsqueeze(1).broadcast_to([P, TB, VH]),
                                               ALU.mult, ALU.mult).then_inc(self.g_g_ready, 1)

            def gates_pool(self, pool):
                pool.wait_ge(self.g_beta1, 1)
                nc.gpsimd.tensor_tensor(self.s_beta[:, :, :], self.s_beta[:, :, :],
                                        minus1[:, 0:TB * VH].rearrange("p (t h) -> p t h", t=TB), ALU.pow).then_inc(self.g_beta_ready, 1)

            def pairs_pe(self, pe, s):
                if s < 16:
                    u = self.unit + s
                    gi = self.qkv + s // 2
                    free_unit(pe, u)
                    for tb in range(TB):
                        pe.wait_ge(acc_free[gi % 2][tb], gi // 2 + 1)
                    for c in range(2):
                        for tb in range(TB):
                            mm = nc.tensor.transpose(tr[u % 2][:, c * SEQ + tb * P:c * SEQ + (tb + 1) * P],
                                                     prod[gi % 2][tb][:, (2 * (s % 2) + c) * P:(2 * (s % 2) + c + 1) * P], ident[:, :])
                    mm.then_inc(tr_ready, 1)
                if 1 <= s <= 16:
                    pe.wait_ge(self.g_silu, s)
                    if s >= 2:
                        pe.wait_ge(self.g_t2out, s - 1)
                    for tb in range(TB):
                        for c in range(2):
                            mm = nc.tensor.transpose(aux[0][:, tb * 256 + c * P:tb * 256 + (c + 1) * P],
                                                     self.cv[(s - 1) % 2][:, c * SEQ + tb * P:c * SEQ + (tb + 1) * P], ident[:, :])
                    mm.then_inc(self.g_t2, 1)
                if 2 <= s < 10:
                    p = s - 2
                    pe.wait_ge(self.g_t2out, p + 1)
                    if p:
                        pe.wait_ge(self.g_t3out, p)
                    else:
                        pe.wait_ge(self.g_eg_ready, 2)
                    for c in range(2):
                        for tb in range(TB):
                            src = self.qt[:, tb * 256 + c * P:tb * 256 + (c + 1) * P] if p < 4 else self.kt[:, tb, 2 * (p - 4) + c, :]
                            mm = nc.tensor.transpose(aux[1][:, c * SEQ + tb * P:c * SEQ + (tb + 1) * P], src, ident[:, :])
                    mm.then_inc(self.g_t3, 1)

            def pairs_act(self, act, s):
                if s < 16:
                    u = self.unit + s
                    act.wait_ge(tr_ready, u + 1)
                    if s >= 2:
                        act.wait_ge(self.g_t2, s - 1)
                    for c in range(2):
                        nc.scalar.activation(self.cv[s % 2][:, c * SEQ:(c + 1) * SEQ], tr[u % 2][:, c * SEQ:(c + 1) * SEQ],
                                             ACT.Copy, scale=vcol("gdn_conv", 3 * 32 + 2 * s + c)).then_inc(self.g_tap3, 1)
                if 1 <= s <= 8:
                    act.wait_ge(self.g_t2, s)
                    if s >= 2:
                        act.wait_ge(self.g_t2red, s - 1)
                    nc.scalar.activation(self.sq[:, :], aux[0][:, :], ACT.Square).then_inc(self.g_t2sq, 1)
                if 2 <= s < 10:
                    p = s - 2
                    act.wait_ge(self.g_t3, p + 1)
                    dst = (self.qf if p < 4 else self.kf)[:, 2 * (p % 4):2 * (p % 4) + 2, :].rearrange("p c t -> p (c t)")
                    nc.scalar.activation(dst, aux[1][:, :], ACT.Copy).then_inc(self.g_t3out, 1)
                if s < 16:
                    act.wait_ge(tr_free[(self.unit + s) % 2], (self.unit + s) // 2 + 1)
                    nc.scalar.activation(self.cv[s % 2][:, :], self.cv[s % 2][:, :], ACT.Silu).then_inc(self.g_silu, 1)

            def pairs_dve(self, dve, s):
                if s < 16:
                    u = self.unit + s
                    dve.wait_ge(self.g_tap3, 2 * s + 2)
                    for k in range(1, 4):
                        for c in range(2):
                            o = self.cv[s % 2][:, c * SEQ + k:(c + 1) * SEQ]
                            if k > 1:
                                dve.wait_ge(self.g_taps, 5 * s + 2 * (k - 2) + c + 1)
                            x = nc.vector.scalar_tensor_tensor(o, tr[u % 2][:, c * SEQ:(c + 1) * SEQ - k],
                                                               vcol("gdn_conv", (3 - k) * 32 + 2 * s + c), o, ALU.mult, ALU.add)
                            x.then_inc(tr_free[u % 2] if (k, c) == (3, 1) else self.g_taps, 1)
                if 1 <= s <= 16:
                    p = s - 1
                    src = aux[0][:, :].rearrange("p (t c d) -> p t c d", t=TB, c=2)
                    if p < 8:
                        dve.wait_ge(self.g_t2sq, p + 1)
                        nc.vector.tensor_reduce(self.ss[:, :], self.sq[:, :].rearrange("p (n d) -> p n d", n=4), AX.X,
                                                ALU.add).then_inc(self.g_t2red, 1)
                        dve.wait_ge(self.g_t2red, p + 1)
                        f = float(HEAD) if p < 4 else 1.0
                        nc.vector.tensor_scalar(self.ss[:, :], self.ss[:, :], f, EPS * f, ALU.mult, ALU.add).then_inc(self.g_t2ms, 1)
                        dve.wait_ge(self.g_t2rn, p + 1)
                        rn = self.rn[:, :].rearrange("p (t c) -> p t c", t=TB).unsqueeze(3).broadcast_to([P, TB, 2, P])
                        if p < 4:
                            if p:
                                dve.wait_ge(self.g_t3, p)
                            dst = self.qt[:, :].rearrange("p (t c d) -> p t c d", t=TB, c=2)
                        else:
                            dst = self.kt[:, :, 2 * (p - 4):2 * (p - 4) + 2, :]
                    else:
                        h = 2 * (p - 8)
                        dve.wait_ge(self.g_t2, p + 1)
                        dve.wait_ge(self.g_beta_ready, 1)
                        rn = self.s_beta[:, :, h:h + 2].unsqueeze(3).broadcast_to([P, TB, 2, P])
                        dst = self.vb[:, :, h:h + 2, :]
                    nc.vector.tensor_tensor(dst, src, rn, ALU.mult).then_inc(self.g_t2out, 1)

            def pairs_pool(self, pool, s):
                if 1 <= s <= 8:
                    pool.wait_ge(self.g_t2ms, s)
                    nc.gpsimd.tensor_tensor(self.rn[:, :], self.ss[:, :], mhalf[:, 0:4], ALU.pow).then_inc(self.g_t2rn, 1)

            def pe(self, pe):
                prenorm_pe(pe, self.n, self.norm_unit)
                products(pe, self.ba, xh, xl, before=wait_x(pe, self.norm_unit))
                products(pe, self.qkv, xh, xl)
                pe.wait_ge(self.g_g_ready, 1)
                nc.tensor.matmul(aux[1][:, 0:VH], upto[:, :], self.s_g[:, 1, :], start=True, stop=True)
                nc.tensor.matmul(aux[1][:, VH:2 * VH], beyond[:, :], self.s_g[:, 0, :], start=True, stop=True).then_inc(self.g_G_psum, 1)
                for g in range(1, 8):
                    products(pe, self.qkv + g, xh, xl, before=lambda k0, kn: self.pairs_pe(pe, 2 * g - 2) if k0 else None)
                    self.pairs_pe(pe, 2 * g - 1)
                for s in range(14, 18):
                    self.pairs_pe(pe, s)
                for B in range(self.NB):
                    self.core_pe(pe, B)
                pe.wait_ge(self.g_o_ready, self.NB)
                for g in range(4):
                    products(pe, self.z + g, xh, xl)
                    if g:
                        self.turn_pe(pe, g - 1)
                self.turn_pe(pe, 3)

                def split(k0, kn):
                    for u in (self.zunit + k0 // 2, self.zunit + k0 // 2 + 1):
                        pe.wait_ge(tr_free[u % 2], u // 2 + 1)
                products(pe, self.out, hh, hl, before=split)
                products(pe, self.out + 1, hh, hl)

            def act(self, act):
                prenorm_act(act, self.n, self.norm_unit, self.g0)
                stream_act(act, self.ba)
                for g in range(8):
                    gi = self.qkv + g
                    if g == 1:
                        self.gates_act(act)
                    t = tile_of[gi]
                    split_high(act, t + 2)
                    if g:
                        self.pairs_act(act, 2 * g - 2)
                    split_high(act, t + 3)
                    for tb in range(TB):
                        act.wait_ge(acc_ready, 2 * gi + tb + 1)
                        nc.scalar.activation(prod[gi % 2][tb][:, :], acc[gi % 2][tb][:, :],
                                             ACT.Copy).then_inc(acc_free[gi % 2][tb], 1)
                    if g:
                        self.pairs_act(act, 2 * g - 1)
                for s in range(14, 18):
                    self.pairs_act(act, s)
                for B in range(self.NB):
                    self.core_act(act, B)
                act.wait_ge(self.g_o_ready, self.NB)
                for tb in range(TB):
                    nc.scalar.activation(self.osq[:, tb], self.vb[:, tb], ACT.Square).then_inc(self.g_osq_ready, 1)
                for g in range(4):
                    gi = self.z + g
                    stream_act(act, gi)
                    for tb in range(TB):
                        act.wait_ge(acc_ready, 2 * gi + tb + 1)
                        nc.scalar.activation(prod[gi % 2][tb][:, :], acc[gi % 2][tb][:, :],
                                             ACT.Silu).then_inc(acc_free[gi % 2][tb], 1)
                    if g:
                        self.turn_act(act, g - 1)
                self.turn_act(act, 3)
                stream_act(act, self.out)
                postnorm_act(act, self.post, self.out)

            def dve(self, dve):
                prenorm_dve(dve, self.n, self.norm_unit, self.g0)
                stream_dve(dve, self.ba)
                for g in range(8):
                    if g == 1:
                        self.gates_dve(dve)
                        dve.wait_ge(self.g_beta_ready, 1)
                        dve.wait_ge(self.g_eg_ready, 2)
                        nc.vector.scalar_tensor_tensor(self.s_nbe[:, :], self.s_beta[:, 1, :], -1.0, self.s_eg[:, :],
                                                       ALU.mult, ALU.mult).then_inc(self.g_nbe_ready, 1)
                    t = tile_of[self.qkv + g]
                    if g:
                        self.pairs_dve(dve, 2 * g - 2)
                    split_low(dve, t + 2)
                    split_low(dve, t + 3)
                    if g:
                        self.pairs_dve(dve, 2 * g - 1)
                for s in range(14, 18):
                    self.pairs_dve(dve, s)
                for B in range(self.NB):
                    self.core_dve(dve, B)
                for tb in range(TB):
                    dve.wait_ge(self.g_osq_ready, tb + 1)
                    nc.vector.tensor_reduce(self.oss[:, tb, :], self.osq[:, tb], AX.X, ALU.add).then_inc(self.g_ored, 1)
                dve.wait_ge(self.g_ored, TB)
                nc.vector.tensor_scalar(self.oss[:, :, :], self.oss[:, :, :], 1.0 / HEAD, EPS, ALU.mult, ALU.add).then_inc(self.g_oms, 1)
                dve.wait_ge(self.g_orn_ready, 1)
                for g in range(4):
                    stream_dve(dve, self.z + g)
                    for tb in range(TB):
                        o = self.vb[:, tb, 4 * g:4 * g + 4, :]
                        nc.vector.tensor_tensor(o, o, self.orn[:, tb, 4 * g:4 * g + 4].unsqueeze(2).broadcast_to([P, 4, P]),
                                                ALU.mult).then_inc(self.g_o_normed, 1)
                    if g:
                        self.turn_dve(dve, g - 1)
                self.turn_dve(dve, 3)
                postnorm_dve(dve, self.post, self.out, 1.0)

            def pool(self, pool):
                prenorm_pool(pool, self.n)
                for g in range(8):
                    if g == 1:
                        self.gates_pool(pool)
                    if g:
                        self.pairs_pool(pool, 2 * g - 2)
                        self.pairs_pool(pool, 2 * g - 1)
                for s in range(14, 18):
                    self.pairs_pool(pool, s)
                for B in range(self.NB):
                    self.core_pool(pool, B)
                pool.wait_ge(self.g_oms, 1)
                nc.gpsimd.tensor_tensor(self.orn[:, :, :], self.oss[:, :, :], mhalf[:, 0:TB * VH].rearrange("p (t h) -> p t h", t=TB),
                                        ALU.pow).then_inc(self.g_orn_ready, 1)
                for g in range(4):
                    gi = self.z + g
                    for tb in range(TB):
                        pool.wait_ge(acc_free[gi % 2][tb], gi // 2 + 1)
                        pool.wait_ge(self.g_o_normed, 2 * g + tb + 1)
                        o = self.vb[:, tb, 4 * g:4 * g + 4, :].rearrange("p h d -> p (h d)")
                        nc.gpsimd.tensor_tensor(o, o, prod[gi % 2][tb][:, :], ALU.mult).then_inc(self.g_o_gated, 1)
                postnorm_pool(pool, self.post, self.out)

            def turn_pe(self, pe, g):
                pe.wait_ge(self.g_o_gated, 2 * g + 2)
                for h in range(2):
                    u = self.zunit + 2 * g + h
                    free_unit(pe, u)
                    for c in range(2):
                        for tb in range(TB):
                            mm = nc.tensor.transpose(tr[u % 2][:, c * SEQ + tb * P:c * SEQ + (tb + 1) * P],
                                                     self.vb[:, tb, 4 * g + 2 * h + c, :], ident[:, :])
                    mm.then_inc(tr_ready, 1)

            def turn_act(self, act, g):
                for h in range(2):
                    u = self.zunit + 2 * g + h
                    act.wait_ge(tr_ready, u + 1)
                    nc.scalar.activation(hh[:, 4 * g + 2 * h:4 * g + 2 * h + 2, :].rearrange("p c t -> p (c t)"), tr[u % 2][:, :],
                                         ACT.Copy, scale=vcol("gdn_norm", 0)).then_inc(self.g_zhh, 1)

            def turn_dve(self, dve, g):
                for h in range(2):
                    u = self.zunit + 2 * g + h
                    dve.wait_ge(self.g_zhh, 2 * g + h + 1)
                    s = slice(4 * g + 2 * h, 4 * g + 2 * h + 2)
                    nc.vector.scalar_tensor_tensor(hl[:, s, :].rearrange("p c t -> p (c t)"), tr[u % 2][:, :], vcol("gdn_norm", 0),
                                                   hh[:, s, :].rearrange("p c t -> p (c t)").bitcast(F32),
                                                   ALU.mult, ALU.subtract).then_inc(tr_free[u % 2], 1)

            def core_pe(self, pe, B):
                bKK, bQK, bD, bDT = tr[0], tr[1], (acc[1][0], acc[1][1]), (acc[0][0], acc[0][1])
                bV, bS, bKS, bQS, bO = aux[1], tr[0], acc[1][0], acc[1][1], (tr[0], tr[1])
                if B == 0:
                    pe.wait_ge(self.g_t3out, 8)
                    pe.wait_ge(self.g_t2out, 16)
                    for i in range(2):
                        gi = self.qkv + 6 + i
                        for tb in range(TB):
                            pe.wait_ge(acc_free[gi % 2][tb], gi // 2 + 1)
                        u = self.unit + 14 + i
                        pe.wait_ge(tr_free[u % 2], u // 2 + 1)
                else:
                    pe.wait_ge(self.g_o_ready, B)
                for a in range(2):
                    for tb in range(TB):
                        kf = self.kf[:, 2 * B + a, tb * P:(tb + 1) * P]
                        qf = self.qf[:, 2 * B + a, tb * P:(tb + 1) * P]
                        c = slice((2 * a + tb) * P, (2 * a + tb + 1) * P)
                        nc.tensor.matmul(bKK[:, c], kf, kf, start=True, stop=True)
                        mm = nc.tensor.matmul(bQK[:, c], kf, qf, start=True, stop=True)
                mm.then_inc(self.g_kk, 1)
                pe.wait_ge(self.g_gm_ready, 8 * B + 8)
                for a in range(2):
                    mm = nc.tensor.matmul(bD[a][:, :], upto[:, :], self.gm[:, 4 * a:4 * a + 4, :].rearrange("p j s -> p (j s)"),
                                          start=True, stop=True)
                mm.then_inc(self.g_D_psum, 1)
                for a in range(2):
                    for j in range(4):
                        mm = nc.tensor.matmul(bDT[a][:, j * P:(j + 1) * P], self.gm[:, 4 * a + j, :], upto[:, :], start=True, stop=True)
                mm.then_inc(self.g_D_psum, 1)
                keep_clock(pe, 5)
                pe.wait_ge(self.g_A_ready, 8 * B + 8)
                pe.wait_ge(self.g_DT_ready, 2 * B + 2)
                self.inv.pe(pe, B)
                pe.wait_ge(self.inv.u_ready, 14 * (B + 1))
                for v in range(4):
                    mm = nc.tensor.matmul(bV[:, v * P:(v + 1) * P], self.U[:, 2 * v, :], self.vb[:, 0, 4 * B + v, :], start=True, stop=True)
                mm.then_inc(self.g_v0_psum, 1)
                keep_clock(pe, 7, acc[0][0])
                pe.wait_ge(self.g_vt_ready, 4 * B + 4)
                pe.wait_ge(self.g_qk_ready, B + 1)
                for a in range(2):
                    mm = nc.tensor.matmul(bS[:, a * 256:(a + 1) * 256], self.kt[:, 0, 2 * B + a, :],
                                          self.vt[:, 2 * a:2 * a + 2, :].rearrange("p v e -> p (v e)"), start=True, stop=True)
                mm.then_inc(self.g_S_psum, 1)
                keep_clock(pe, 3, acc[0][0])
                pe.wait_ge(self.g_S_ready, B + 1)
                for a in range(2):
                    s_ = self.S[:, 2 * a:2 * a + 2, :].rearrange("p v e -> p (v e)")
                    nc.tensor.matmul(bKS[:, a * 256:(a + 1) * 256], self.kf[:, 2 * B + a, P:], s_, start=True, stop=True)
                    mm = nc.tensor.matmul(bQS[:, a * 256:(a + 1) * 256], self.qf[:, 2 * B + a, P:], s_, start=True, stop=True)
                mm.then_inc(self.g_kS_psum, 1)
                keep_clock(pe, 6, acc[0][0])
                pe.wait_ge(self.g_r_ready, 4 * B + 4)
                for v in range(4):
                    mm = nc.tensor.matmul(bV[:, v * P:(v + 1) * P], self.U[:, 2 * v + 1, :], self.vt[:, v, :], start=True, stop=True)
                mm.then_inc(self.g_v1_psum, 1)
                for v in range(4):
                    mm = nc.tensor.matmul(bO[0][:, v * P:(v + 1) * P], self.qk[:, 2 * v, :], self.vn[:, 0, v, :], start=True, stop=True)
                mm.then_inc(self.g_o_psum, 1)
                pe.wait_ge(self.g_v1_ready, B + 1)
                for v in range(4):
                    mm = nc.tensor.matmul(bO[1][:, v * P:(v + 1) * P], self.qk[:, 2 * v + 1, :], self.vn[:, 1, v, :], start=True, stop=True)
                mm.then_inc(self.g_o_psum, 1)

            def core_act(self, act, B):
                bD, bDT = (acc[1][0], acc[1][1]), (acc[0][0], acc[0][1])
                act.wait_ge(self.g_D_psum, 2 * B + 1)
                if B:
                    act.wait_ge(self.g_o_psum, 2 * B)
                for a in range(2):
                    nc.scalar.activation(self.A[:, 4 * a:4 * a + 4, :].rearrange("p j s -> p (j s)"), bD[a][:, :], ACT.Exp).then_inc(self.g_D_ready, 1)
                act.wait_ge(self.g_D_psum, 2 * B + 2)
                for a in range(2):
                    nc.scalar.activation(self.qk[:, 4 * a:4 * a + 4, :].rearrange("p j s -> p (j s)"), bDT[a][:, :], ACT.Exp).then_inc(self.g_DT_ready, 1)
                self.inv.act(act, B)
                act.wait_ge(self.g_v0_psum, B + 1)
                nc.scalar.activation(self.vn[:, 0].rearrange("p v e -> p (v e)"), aux[1][:, :], ACT.Copy).then_inc(self.g_v0_ready, 1)
                act.wait_ge(self.g_S_psum, B + 1)
                nc.scalar.activation(self.S[:, :, :].rearrange("p v e -> p (v e)"), tr[0][:, :], ACT.Copy).then_inc(self.g_S_ready, 1)
                act.wait_ge(self.g_kS_psum, B + 1)
                for v in range(4):
                    nc.scalar.activation(self.qS[:, v, :], acc[1][1][:, v * P:(v + 1) * P], ACT.Copy,
                                         scale=self.s_eg[:, 4 * B + v:4 * B + v + 1]).then_inc(self.g_qS_ready, 1)
                act.wait_ge(self.g_v1_psum, B + 1)
                nc.scalar.activation(self.vn[:, 1].rearrange("p v e -> p (v e)"), aux[1][:, :], ACT.Copy).then_inc(self.g_v1_ready, 1)

            def core_dve(self, dve, B):
                dve.wait_ge(self.g_kk, B + 1)
                for a in range(2):
                    dve.wait_ge(self.g_D_ready, 2 * B + a + 1)
                    for v in range(2):
                        for tb in range(TB):
                            j = 4 * a + 2 * v + tb
                            nc.vector.scalar_tensor_tensor(
                                self.A[:, j, :], tr[0][:, (2 * a + tb) * P:(2 * a + tb + 1) * P],
                                self.s_beta[:, tb, 4 * B + 2 * a + v:4 * B + 2 * a + v + 1],
                                self.A[:, j, :], ALU.mult, ALU.mult).then_inc(self.g_A_ready, 1)
                self.inv.dve(dve, B)
                dve.wait_ge(self.g_DT_masked, B + 1)
                for a in range(2):
                    o = self.qk[:, 4 * a:4 * a + 4, :].rearrange("p (v t) s -> p v t s", v=2)
                    x = nc.vector.tensor_tensor(o, o, tr[1][:, 2 * a * P:(2 * a + 2) * P].rearrange("p (t s) -> p t s", t=TB).unsqueeze(1)
                                                .broadcast_to([P, 2, TB, P]), ALU.mult)
                x.then_inc(self.g_qk_ready, 1)
                dve.wait_ge(self.g_v0_ready, B + 1)
                if B:
                    dve.wait_ge(self.g_v1_psum, B)
                for v in range(4):
                    nc.vector.tensor_scalar(self.vt[:, v, :], self.vn[:, 0, v, :], self.s_etail[:, 4 * B + v:4 * B + v + 1], None,
                                            ALU.mult).then_inc(self.g_vt_ready, 1)
                dve.wait_ge(self.g_S_psum, B + 1)
                dve.wait_ge(self.g_kS_psum, B + 1)
                for v in range(4):
                    nc.vector.scalar_tensor_tensor(self.vt[:, v, :], acc[1][0][:, v * P:(v + 1) * P],
                                                   self.s_nbe[:, 4 * B + v:4 * B + v + 1], self.vb[:, 1, 4 * B + v, :],
                                                   ALU.mult, ALU.add).then_inc(self.g_r_ready, 1)
                dve.wait_ge(self.g_o_psum, 2 * B + 1)
                nc.vector.tensor_copy(self.vb[:, 0, 4 * B:4 * B + 4, :].rearrange("p v e -> p (v e)"), tr[0][:, :]).then_inc(self.g_o_half, 1)
                dve.wait_ge(self.g_o_psum, 2 * B + 2)
                dve.wait_ge(self.g_qS_ready, 4 * B + 4)
                nc.vector.tensor_tensor(self.vb[:, 1, 4 * B:4 * B + 4, :].rearrange("p v e -> p (v e)"), tr[1][:, :],
                                        self.qS[:, :, :].rearrange("p v e -> p (v e)"), ALU.add).then_inc(self.g_o_ready, 1)

            def core_pool(self, pool, B):
                if B:
                    pool.wait_ge(self.g_D_psum, 2 * B)
                else:
                    pool.wait_ge(self.g_t2, 16)
                    pool.wait_ge(self.g_t2red, 8)
                    pool.wait_ge(self.g_t3, 8)
                for j in range(8):
                    a, v, tb = j // 4, j // 2 % 2, j % 2
                    h = 4 * B + 2 * a + v
                    nc.gpsimd.tensor_scalar(self.gm[:, j, :], beyond[:, :], self.s_g[:, tb, h:h + 1], None, ALU.mult).then_inc(self.g_gm_ready, 1)
                self.inv.pool(pool, B)
                pool.wait_ge(self.g_DT_ready, 2 * B + 2)
                nc.gpsimd.tensor_tensor(self.qk[:, :, :], self.qk[:, :, :], upto[:, :].unsqueeze(1).broadcast_to([P, 8, P]),
                                        ALU.mult).then_inc(self.g_DT_masked, 1)

        class Steps:
            def __init__(self, name, order):
                self.sem, self.order, self.n = sem(name), order, 0
                self.at = {x: i + 1 for i, x in enumerate(order)}

            def one(self, name):
                assert self.order[self.n] == name, (self.order[self.n], name)
                self.n += 1
                return 1

        NH, ND = 8, 64
        NC = (SEQ - 32) // 16 + 1

        class Mixer:

            def __init__(self):
                self.q, self.kv, self.kvg, self.rw, self.merge, self.out = (
                    first["mix_" + x] for x in ("q", "kv", "kvg", "rw", "merge", "out"))
                self.proj = [(first[f"mix_pn{j}"], first[f"mix_pr{j}"]) for j in range(2)]
                self.n, self.post = plan["pre"], plan["post"]
                self.norm_unit = plan["unit"]
                u = plan["unit"] + DC // 2
                self.uq, self.uc, self.uk, self.ur, self.uy = u, u + 2, u + 3, u + 4, u + 11
                plan["pre"] += 1
                plan["post"] += 1
                plan["unit"] += DC // 2 + 11 + 4
                self.g0 = lambda c: vcol("norm_mix", c)
                self.small_in = sem("mix_small_in")
                self.w1_in = sem("mix_w1_in")
                self.PE, self.AC, self.DV, self.PL = (Steps("mix_" + x, MIX_ORDER.get(x, [])) for x in ("pe", "act", "dve", "pool"))

                c = Carve(gain_at, 8 * 1024)
                self.wua = c("mix_wua", [512])
                self.gup = c("mix_gup", [512])
                self.w2 = c("mix_w2", [2, P])
                self.cneg = c("mix_cneg", [384])
                self.blk = c("mix_blk", [P])
                self.i64 = c("mix_i64", [P])
                self.st64 = c("mix_st64", [P])
                self.fresh = gate_s[0][0]
                self.omm = gate_s[0][1]

                c = Carve(arena_at, 10 * 4096)
                self.rwf = c("mix_rwf", [14, SEQ])
                self.on = c("mix_on", [4, SEQ])
                mark = c.at
                self.qf = c("mix_qf", [4, SEQ])
                self.kf = c("mix_kf", [2, SEQ])
                self.vt_ = c("mix_vt", [2, TB, P])
                self.S = [[c(f"mix_S{i}{b}", [384]) for b in range(2)] for i in range(2)]
                self.PT = [[c(f"mix_PT{i}{b}", [384]) for b in range(2)] for i in range(2)]
                self.PTc = [c(f"mix_PTc{i}", [256]) for i in range(2)]
                c = Carve(mark, arena_at + 10 * 4096 - mark)
                self.bt, self.kt, self.vt = (c(f"rw_{x}t", [TB, 512]) for x in "bkv")
                self.bonus = c("rw_bonus", [4, SEQ])
                self.g = c("rw_g", [4, SEQ])
                self.cwl = c("rw_cwl", [4, 4])
                self.rinv = c("rw_rinv", [16])
                self.ln = c("rw_ln", [48])
                c = Carve(mark, arena_at + 10 * 4096 - mark)
                self.mg = c("mix_mg", [TB, 2 * D])

                c = Carve(slab_at, 2 * FC * SEQ * 4)
                self.w1 = c("mix_w1", [2, 32, P])
                self.zb = c("mix_zb", [2, 32, NC])
                self.zf = c("mix_zf", [2, SEQ])
                self.hs = c("mix_hs", [2, 16])
                self.kcs, self.kcq, self.kcf = (c("mix_" + x, [16]) for x in ("kcs", "kcq", "kcf"))
                self.krn = c("mix_krn", [16])
                self.vc = c("mix_vc", [P])
                self.cs = c("mix_cs", [TB, NH, NC + 1])
                self.cm, self.csum, self.ccoef = (c("mix_" + x, [TB, NH]) for x in ("cm", "csum", "ccoef"))
                self.cmask, self.cm01 = (c("mix_" + x, [TB, 16]) for x in ("cmask", "cm01"))
                self.gt = c("mix_gt", [TB, 24])
                self.nst, self.nrn = (c("mix_" + x, [TB, 12]) for x in ("nst", "nrn"))
                self.nm, self.sm, self.inv_, self.coef = (c("mix_" + x, [2, 4]) for x in ("nm", "sum", "inv", "coef"))
                c = Carve(work_at, 8 * 1024)
                self.qn = c("mix_qn", [TB, 4, 2, ND])
                self.sq = c("mix_sq", [TB, 512])
                self.kn = self.qn

                c = Carve(slab_at, 2 * FC * SEQ * 4)
                base = c.at
                self.tmp = [c(f"rw_tmp{i}", [4, SEQ]) for i in range(8)]
                c.at = base
                self.A, self.G1, self.RB, self.RK, self.U, self.T = (c("rw_" + x, [8, P]) for x in ("A", "G1", "RB", "RK", "U", "T"))
                self.X = c("rw_X", [8, 64])
                c.at = base + 8 * 4096
                self.al = c("rw_al", [4, SEQ])
                self.rt = c("rw_rt", [4, SEQ])
                self.M = c("rw_M", [2, ND])
                self.N1 = c("rw_N1", [4, ND])
                self.SA = c("rw_SA", [4, ND])
                self.RM = c("rw_RM", [4, ND])
                c = Carve(work_at, 8 * 1024)
                self.be = c("rw_be", [4, SEQ])
                self.ka = c("rw_ka", [4, SEQ])
                c = Carve(work_at, 8 * 1024)
                self.ysq = c("rw_ysq", [TB, NH, ND])
                c = Carve(arena_at, 4096)
                self.y = c("rw_y", [TB, NH, ND])
                c = Carve(slab_at, 2 * FC * SEQ * 4)
                self.gv = c("rw_gv", [TB, 4, ND])
                self.kvs = c("rw_kvs", [4, 2, ND])
                self.inv = Inverse("rw_inv", 8, 6, self.A, self.U, self.T, self.X)

            def sp(self, sp):
                gi = self.q
                for gi in range(self.q, self.out + 2):
                    if gi == self.kv:
                        if self.post:
                            sp.wait_ge(res_ready, 4 * self.post)
                        n = self.small_in
                        sp.dma_start(self.wua[0:64, :], ins["rwkv_w_up_2"][0]).then_inc(n, 16)
                        sp.dma_start(self.wua[64:128, :], ins["rwkv_a_up_2"][0]).then_inc(n, 16)
                        sp.dma_start(self.gup[:, :], ins["rwkv_g_up_2"][0]).then_inc(n, 16)
                        for g in range(2):
                            r = slice(64 * g, 64 * g + 64)
                            sp.dma_start(self.w2[r, :, r], ins["cmp_w2_2"][0].rearrange("c e f -> e c f")).then_inc(n, 16)
                    if gi == self.kvg:
                        for g in range(2):
                            r = slice(64 * g, 64 * g + 64)
                            for c in range(2):
                                sp.dma_start(self.w1[r, c, :, r], ins["cmp_w1_2"][0, c].rearrange("l d e -> d l e")).then_inc(self.w1_in, 16)
                    for t in group_tiles(gi):
                        load(sp, t)

            def bank_done(self, pe, gi):
                for tb in range(TB):
                    pe.wait_ge(acc_free[gi % 2][tb], gi // 2 + 1)

            def turn(self, pe, u, src):
                free_unit(pe, u)
                for c in range(2):
                    for tb in range(TB):
                        mm = nc.tensor.transpose(tr[u % 2][:, c * SEQ + tb * P:c * SEQ + (tb + 1) * P], src(c, tb), ident[:, :])
                mm.then_inc(tr_ready, 1)

            def turn_rw(self, pe, g):
                gi = self.rw + g
                self.bank_done(pe, gi)
                for h in range(2 if g < 3 else 1):
                    self.turn(pe, self.ur + 2 * g + h, lambda c, tb: prod[gi % 2][tb][:, (2 * h + c) * P:(2 * h + c + 1) * P])

            def pe(self, pe):
                PE, AC, DV, PL = self.PE, self.AC, self.DV, self.PL
                prenorm_pe(pe, self.n, self.norm_unit)
                products(pe, self.q, xh, xl, before=wait_x(pe, self.norm_unit))
                products(pe, self.kv, xh, xl)
                for h in range(2):
                    pe.wait_ge(DV.sem, DV.at["qn", 1])
                    self.turn(pe, self.uq + h, lambda c, tb: self.qn[:, tb, 2 * h + c].rearrange("p h d -> p (h d)"))
                products(pe, self.kvg, xh, xl)
                self.turn(pe, self.uc, lambda c, tb: prod[self.kv % 2][tb][:, c * P:(c + 1) * P])
                products(pe, self.rw, xh, xl)
                pe.wait_ge(DV.sem, DV.at["kn"])
                self.turn(pe, self.uk, lambda c, tb: self.kn[:, tb, c].rearrange("p h d -> p (h d)"))
                for g in range(1, 4):
                    products(pe, self.rw + g, xh, xl)
                    self.turn_rw(pe, g - 1)
                self.turn_rw(pe, 3)
                self.nsa_pe(pe)
                self.rwkv_pe(pe)
                for g in range(4):
                    products(pe, self.merge + g, xh, xl)
                for j in range(2):
                    pe.wait_ge(PL.sem, PL.at["on_low"])
                    products(pe, self.proj[j][0], hh, hl)
                    pe.wait_ge(PL.sem, PL.at["or_low"])
                    products(pe, self.proj[j][1], hh[:, 4:8, :], hl[:, 4:8, :])
                for u in range(4):
                    pe.wait_ge(PL.sem, PL.at["y", u // 2])
                    self.turn(pe, self.uy + u, lambda c, tb: work[:, tb, (2 * u + c) * P:(2 * u + c + 1) * P])

                def split(k0, kn):
                    for u in (self.uy + k0 // 2, self.uy + k0 // 2 + 1):
                        pe.wait_ge(tr_free[u % 2], u // 2 + 1)
                products(pe, self.out, hh[:, 8:16, :], hl[:, 8:16, :], before=split)
                products(pe, self.out + 1, hh[:, 8:16, :], hl[:, 8:16, :])

            def to_prod(self, act, gi, cols=GW):
                for tb in range(TB):
                    act.wait_ge(acc_ready, 2 * gi + tb + 1)
                    nc.scalar.activation(prod[gi % 2][tb][:, 0:cols], acc[gi % 2][tb][:, 0:cols],
                                         ACT.Copy).then_inc(acc_free[gi % 2][tb], 1)

            def shift_act(self, act, g):
                for h in range(2 if g < 3 else 1):
                    u = self.ur + 2 * g + h
                    act.wait_ge(tr_ready, u + 1)
                    for c in range(2):
                        ch = 4 * g + 2 * h + c
                        nc.scalar.activation(self.rwf[:, ch, :], tr[u % 2][:, c * SEQ:(c + 1) * SEQ], ACT.Copy,
                                                         scale=self.omm[:, ch:ch + 1]).then_inc(self.AC.sem, self.AC.one(("shift", ch)))

            def act(self, act):
                PE, AC, DV, PL = self.PE, self.AC, self.DV, self.PL
                prenorm_act(act, self.n, self.norm_unit, self.g0)
                stream_act(act, self.q)
                self.to_prod(act, self.q)
                for tb in range(TB):
                    act.wait_ge(acc_free[self.q % 2][tb], self.q // 2 + 1)
                    if tb == 0:
                        PE_x = self.norm_unit + 3
                        act.wait_ge(tr_ready, PE_x + 1)
                    nc.scalar.activation(self.sq[:, tb, :], prod[self.q % 2][tb][:, :], ACT.Square).then_inc(AC.sem, AC.one(("qsq", tb)))
                stream_act(act, self.kv)
                self.to_prod(act, self.kv)
                act.wait_ge(DV.sem, DV.at["qred"])
                for tb in range(TB):
                    act.wait_ge(acc_free[self.kv % 2][tb], self.kv // 2 + 1)
                    nc.scalar.activation(self.sq[:, tb, 0:P], prod[self.kv % 2][tb][:, 256:384], ACT.Square).then_inc(AC.sem, AC.one(("ksq", tb)))
                for h in range(2):
                    u = self.uq + h
                    act.wait_ge(tr_ready, u + 1)
                    nc.scalar.activation(self.qf[:, 2 * h:2 * h + 2, :].rearrange("p c t -> p (c t)"), tr[u % 2][:, :], ACT.Copy,
                                         scale=vcol("qk_gain", 0)).then_inc(tr_free[u % 2], 1)
                stream_act(act, self.kvg)
                self.to_prod(act, self.kvg, 280)
                for tb in range(TB):
                    act.wait_ge(acc_free[self.kvg % 2][tb], self.kvg // 2 + 1)
                    nc.scalar.activation(self.sq[:, tb, P:2 * P], prod[self.kvg % 2][tb][:, 0:P], ACT.Square).then_inc(AC.sem, AC.one(("wsq", tb)))
                for tb in range(TB):
                    nc.scalar.activation(self.gt[:, tb, :], prod[self.kvg % 2][tb][:, 256:280], ACT.Sigmoid).then_inc(AC.sem, AC.one(("gate", tb)))
                act.wait_ge(tr_ready, self.uc + 1)
                nc.scalar.activation(self.zf[:, :, :].rearrange("p c t -> p (c t)"), tr[self.uc % 2][:, :],
                                     ACT.Copy).then_inc(tr_free[self.uc % 2], 1)
                for g in range(4):
                    gi = self.rw + g
                    stream_act(act, gi)
                    if g == 0:
                        act.wait_ge(DV.sem, DV.at["kn"])
                        act.wait_ge(PL.sem, PL.at["v"])
                    self.to_prod(act, gi, width[gi])
                    if g == 0:
                        act.wait_ge(tr_ready, self.uk + 1)
                        for b in range(2):
                            x = nc.scalar.activation(self.kf[:, b, :], tr[self.uk % 2][:, b * SEQ:(b + 1) * SEQ], ACT.Copy,
                                                     scale=vcol("qk_gain", 2 + b))
                            if b:
                                x.then_inc(tr_free[self.uk % 2], 1)
                            else:
                                x.then_inc(AC.sem, AC.one("ksf"))
                    else:
                        self.shift_act(act, g - 1)
                self.shift_act(act, 3)
                self.nsa_act(act)
                self.rwkv_act(act)
                for g in range(4):
                    gi = self.merge + g
                    stream_act(act, gi)
                    for tb in range(TB):
                        act.wait_ge(acc_ready, 2 * gi + tb + 1)
                        nc.scalar.activation(self.mg[:, tb, g * GW:(g + 1) * GW], acc[gi % 2][tb][:, :],
                                             ACT.Sigmoid).then_inc(acc_free[gi % 2][tb], 1)
                    if g == 0:
                        act.wait_ge(PL.sem, PL.at["or"])
                        nc.scalar.activation(hh[:, 0:4, :], self.on[:, :, :], ACT.Copy).then_inc(AC.sem, AC.one("on_high"))
                        nc.scalar.activation(hh[:, 4:8, :], self.rwf[:, 8:12, :], ACT.Copy).then_inc(AC.sem, AC.one("or_high"))
                for j in range(2):
                    stream_act(act, self.proj[j][0])
                    stream_act(act, self.proj[j][1])
                for u in range(4):
                    v = self.uy + u
                    act.wait_ge(tr_ready, v + 1)
                    nc.scalar.activation(hh[:, 8 + 2 * u:10 + 2 * u, :].rearrange("p c t -> p (c t)"), tr[v % 2][:, :],
                                                ACT.Copy).then_inc(AC.sem, AC.one(("y_high", u)))
                add_act(act, self.out)

            def shift_dve(self, dve, g):
                for h in range(2 if g < 3 else 1):
                    u = self.ur + 2 * g + h
                    dve.wait_ge(self.AC.sem, self.AC.at["shift", 4 * g + 2 * h + 1])
                    for c in range(2):
                        ch = 4 * g + 2 * h + c
                        o = self.rwf[:, ch, 1:]
                        x = nc.vector.scalar_tensor_tensor(o, tr[u % 2][:, c * SEQ:(c + 1) * SEQ - 1], vcol("mu", ch), o,
                                                           ALU.mult, ALU.add)
                        if c:
                            x.then_inc(tr_free[u % 2], 1)
                        else:
                            x.then_inc(self.DV.sem, self.DV.one(("shift", ch)))

            def heads_norm(self, dve, name, sq, at_, n, f, eps):
                nc.vector.tensor_reduce(self.nst[:, :, at_:at_ + n], sq.rearrange("p t (h d) -> p t h d", d=ND),
                                                    AX.X, ALU.add).then_inc(self.DV.sem, self.DV.one(name + "red"))
                dve.wait_ge(self.DV.sem, self.DV.at[name + "red"])
                nc.vector.tensor_scalar(self.nst[:, :, at_:at_ + n], self.nst[:, :, at_:at_ + n], f, eps,
                                                    ALU.mult, ALU.add).then_inc(self.DV.sem, self.DV.one(name + "ms"))

            def dve(self, dve):
                PE, AC, DV, PL = self.PE, self.AC, self.DV, self.PL
                prenorm_dve(dve, self.n, self.norm_unit, self.g0)
                if self.post:
                    dve.wait_ge(res_ready, 4 * self.post)
                nc.vector.tensor_scalar(self.omm[:, 0:14], vec[:, col["mu"][0] * P + col["mu"][1]:col["mu"][0] * P + col["mu"][1] + 14],
                                               -1.0, 1.0, ALU.mult, ALU.add).then_inc(DV.sem, DV.one("omm"))
                v = nc.vector
                v.memset(self.blk[:, :], 0.0).then_inc(DV.sem, DV.one("blk0"))
                v.tensor_copy(self.i64[:, :], upto[:, :]).then_inc(DV.sem, DV.one("i64_0"))
                v.memset(self.w2[0:64, :, 64:128], 0.0).then_inc(DV.sem, DV.one("w2a"))
                v.memset(self.w2[64:128, :, 0:64], 0.0).then_inc(DV.sem, DV.one("w2b"))
                dve.wait_ge(DV.sem, DV.at["w2b"])
                v.memset(self.blk[0:64, 0:64], 1.0).then_inc(DV.sem, DV.one("blk1"))
                v.memset(self.blk[64:128, 64:128], 1.0).then_inc(DV.sem, DV.one("blk"))
                v.memset(self.i64[0:64, 64:128], 0.0).then_inc(DV.sem, DV.one("i64"))
                stream_dve(dve, self.q)
                dve.wait_ge(AC.sem, AC.at["qsq", 1])
                self.heads_norm(dve, "q", self.sq[:, :, :], 0, 8, 1.0, 64 * EPS)
                dve.wait_ge(PL.sem, PL.at["qrn"])
                for tb in range(TB):
                    nc.vector.tensor_tensor(self.qn[:, tb].rearrange("p c g d -> p g c d"),
                                                   prod[self.q % 2][tb][:, :].rearrange("p (g c d) -> p g c d", g=2, c=4),
                                                   self.nrn[:, tb, 0:8].rearrange("p (g c) -> p g c", g=2).unsqueeze(3).broadcast_to([P, 2, 4, ND]),
                                                   ALU.mult).then_inc(DV.sem, DV.one(("qn", tb)))
                stream_dve(dve, self.kv)
                v.memset(self.w1[0:64, :, :, 64:128], 0.0).then_inc(DV.sem, DV.one("w1a"))
                v.memset(self.w1[64:128, :, :, 0:64], 0.0).then_inc(DV.sem, DV.one("w1b"))
                stream_dve(dve, self.kvg)
                dve.wait_ge(AC.sem, AC.at["wsq", 1])
                self.heads_norm(dve, "k", self.sq[:, :, 0:2 * P], 8, 4, 1.0 / ND, EPS)
                dve.wait_ge(PL.sem, PL.at["krn"])
                for h in range(2):
                    dve.wait_ge(tr_free[(self.uq + h) % 2], (self.uq + h) // 2 + 1)
                for b, src in enumerate((prod[self.kv % 2], prod[self.kvg % 2])):
                    o = 256 if b == 0 else 0
                    for tb in range(TB):
                        nc.vector.tensor_tensor(self.kn[:, tb, b], src[tb][:, o:o + P].rearrange("p (h d) -> p h d", h=2),
                                                       self.nrn[:, tb, 8 + 2 * b:10 + 2 * b].unsqueeze(2).broadcast_to([P, 2, ND]),
                                                       ALU.mult).then_inc(DV.sem, DV.one(("kn", b, tb) if (b, tb) != (1, 1) else "kn"))
                dve.wait_ge(tr_free[self.uc % 2], self.uc // 2 + 1)
                for c in range(2):
                    for a in range(2):
                        z = self.zf[:, c, :].rearrange("p (m r) -> p r m", r=16)[:, :, a:a + NC]
                        at_ = col["cmp_pe"][0] * P + c * 32 + 16 * a
                        nc.vector.tensor_tensor(self.zb[:, c, 16 * a:16 * a + 16, :], z,
                                                       vec[:, at_:at_ + 16].unsqueeze(2).broadcast_to([P, 16, NC]), ALU.add).then_inc(DV.sem, DV.one(("zb", c, a)))
                for g in range(4):
                    stream_dve(dve, self.rw + g)
                    if g:
                        self.shift_dve(dve, g - 1)
                self.shift_dve(dve, 3)
                self.nsa_dve(dve)
                self.rwkv_dve(dve)
                for g in range(4):
                    stream_dve(dve, self.merge + g)
                for j in range(2):
                    for b in range(2):
                        gi = self.proj[j][b]
                        stream_dve(dve, gi)
                        for tb in range(TB):
                            dve.wait_ge(acc_ready, 2 * gi + tb + 1)
                            if j == 0 and b == 0 and tb == 0:
                                dve.wait_ge(acc_free[(self.merge + 3) % 2][1], (self.merge + 3) // 2 + 1)
                            if b:
                                dst = prod[j][tb][:, :]
                            else:
                                dst = work[:, tb, j * GW:(j + 1) * GW]
                            nc.vector.tensor_tensor(dst, acc[gi % 2][tb][:, :], self.mg[:, tb, b * D + j * GW:b * D + (j + 1) * GW],
                                                    ALU.mult).then_inc(acc_free[gi % 2][tb], 1)
                for u in range(4):
                    v = self.uy + u
                    dve.wait_ge(AC.sem, AC.at["y_high", u])
                    s_ = slice(8 + 2 * u, 10 + 2 * u)
                    nc.vector.tensor_tensor(hl[:, s_, :].rearrange("p c t -> p (c t)"), tr[v % 2][:, :],
                                            hh[:, s_, :].rearrange("p c t -> p (c t)").bitcast(F32), ALU.subtract).then_inc(tr_free[v % 2], 1)
                stream_dve(dve, self.out)
                stream_dve(dve, self.out + 1)
                add_dve(dve, self.out)

            def pool(self, pool):
                PE, AC, DV, PL = self.PE, self.AC, self.DV, self.PL
                prenorm_pool(pool, self.n)
                if self.post:
                    pool.wait_ge(res_ready, 4 * self.post)
                pool.wait_ge(DV.sem, DV.at["qms"])
                nc.gpsimd.tensor_tensor(self.nrn[:, :, 0:8], self.nst[:, :, 0:8],
                                               mhalf[:, 0:16].rearrange("p (t h) -> p t h", t=TB), ALU.pow).then_inc(PL.sem, PL.one("qrn"))
                m = nc.gpsimd
                m.memset(self.fresh[:, :], 1.0).then_inc(PL.sem, PL.one("fresh1"))
                m.memset(self.cneg[:, :], 0.0).then_inc(PL.sem, PL.one("cneg0"))
                m.memset(self.cmask[:, :, :], 0.0).then_inc(PL.sem, PL.one("cmask0"))
                m.memset(self.cm01[:, :, :], 1.0).then_inc(PL.sem, PL.one("cm01_0"))
                pool.wait_ge(PL.sem, PL.at["cm01_0"])
                m.memset(self.fresh[:, :].rearrange("p (c r) -> p c r", r=64)[:, :, 0:1], 0.0).then_inc(PL.sem, PL.one("fresh"))
                for b in (0, 2):
                    m.affine_select(out=self.cneg[:, b * P:(b + 1) * P], in_=self.cneg[:, b * P:(b + 1) * P], compare_op=ALU.is_ge,
                                           fill=-1e30, base=0, pattern=[[-1, P]], channel_multiplier=1).then_inc(PL.sem, PL.one(("cneg", b)))
                for x, fill in ((self.cmask, -1e30), (self.cm01, 0.0)):
                    m.affine_select(out=x[:, :, :], in_=x[:, :, :], compare_op=ALU.is_ge, fill=fill, base=-31,
                                           pattern=[[P, TB], [-16, 16]], channel_multiplier=1).then_inc(PL.sem, PL.one(("cm", fill)))
                pool.wait_ge(DV.sem, DV.at["i64"])
                m.affine_select(out=self.st64[:, :], in_=self.i64[:, :], compare_op=ALU.is_gt, fill=0.0, base=0,
                                       pattern=[[1, P]], channel_multiplier=-1).then_inc(PL.sem, PL.one("masks"))
                pool.wait_ge(DV.sem, DV.at["kms"])
                m.tensor_tensor(self.nrn[:, :, 8:12], self.nst[:, :, 8:12],
                                       mhalf[:, 0:8].rearrange("p (t h) -> p t h", t=TB), ALU.pow).then_inc(PL.sem, PL.one("krn"))
                for b, (gi, o) in enumerate(((self.kv, 384), (self.kvg, 128))):
                    for tb in range(TB):
                        pool.wait_ge(acc_free[gi % 2][tb], gi // 2 + 1)
                        m.tensor_copy(self.vt_[:, b, tb, :], prod[gi % 2][tb][:, o:o + P]).then_inc(PL.sem, PL.one(("v", b, tb) if (b, tb) != (1, 1) else "v"))
                self.nsa_pool(pool)
                self.rwkv_pool(pool)
                pool.wait_ge(AC.sem, AC.at["on_high"])
                m.tensor_tensor(hl[:, 0:4, :], self.on[:, :, :], hh[:, 0:4, :].bitcast(F32), ALU.subtract).then_inc(PL.sem, PL.one("on_low"))
                pool.wait_ge(AC.sem, AC.at["or_high"])
                m.tensor_tensor(hl[:, 4:8, :], self.rwf[:, 8:12, :], hh[:, 4:8, :].bitcast(F32), ALU.subtract).then_inc(PL.sem, PL.one("or_low"))
                for j in range(2):
                    gi = self.proj[j]
                    for tb in range(TB):
                        for b in range(2):
                            pool.wait_ge(acc_free[gi[b] % 2][tb], gi[b] // 2 + 1)
                        o = work[:, tb, j * GW:(j + 1) * GW]
                        m.tensor_tensor(o, o, prod[j][tb][:, :], ALU.add).then_inc(PL.sem, PL.one(("y", j, tb) if tb == 0 else ("y", j)))

            def nsa_pe(self, pe):
                PE, AC, DV, PL = self.PE, self.AC, self.DV, self.PL
                pe.wait_ge(self.w1_in, 64)
                pe.wait_ge(DV.sem, DV.at["w1b"])
                pe.wait_ge(DV.sem, DV.at["zb", 1, 1])
                pe.wait_ge(acc_free[(self.rw + 3) % 2][1], (self.rw + 3) // 2 + 1)
                for v in (self.ur + 5, self.ur + 6):
                    pe.wait_ge(tr_free[v % 2], v // 2 + 1)
                for c in range(2):
                    for l in range(32):
                        mm = nc.tensor.matmul(aux[0][:, c * 16:c * 16 + NC], self.w1[:, c, l, :], self.zb[:, c, l, :], start=(l == 0), stop=(l == 31))
                mm.then_inc(PE.sem, PE.one("hid"))
                pe.wait_ge(AC.sem, AC.at["hs"])
                pe.wait_ge(self.small_in, 80)
                pe.wait_ge(PL.sem, PL.at["masks"])
                nc.tensor.matmul(aux[1][:, 0:NC], self.w2[:, 0, :], self.hs[:, 0, 0:NC], start=True, stop=True)
                nc.tensor.matmul(aux[1][0:NC, P:2 * P], self.hs[:, 1, 0:NC], self.w2[:, 1, :], start=True, stop=True).then_inc(PE.sem, PE.one("kvc"))
                pe.wait_ge(AC.sem, AC.at["kcq"])
                nc.tensor.matmul(aux[0][:, 64:64 + NC], self.blk[:, :], self.kcq[:, 0:NC], start=True, stop=True).then_inc(PE.sem, PE.one("kcss"))
                pe.wait_ge(DV.sem, DV.at["kcf"])
                for g in range(2):
                    bank = (acc[0][0], aux[0])[g]
                    r = slice(64 * g, 64 * g + 64)
                    for tb in range(TB):
                        for c in range(4):
                            o = (tb * 4 + c) * 16
                            mm = nc.tensor.matmul(bank[:, o:o + NC], self.qf[r, c, tb * P:(tb + 1) * P], self.kcf[r, 0:NC], start=True, stop=True)
                mm.then_inc(PE.sem, PE.one("csc"))
                self.scores_pe(pe, 0)
                for u in range(8):
                    if u < 7:
                        self.scores_pe(pe, u + 1)
                    pe.wait_ge(DV.sem, DV.at["Pc"])
                    keep_clock(pe, 8, acc[0][0])
                    pe.wait_ge(DV.sem, DV.at["P", u])
                    if u:
                        pe.wait_ge(AC.sem, AC.at["PT", u - 1])
                    for b in range(2):
                        s_ = self.S[u % 2][b]
                        for k in range(3):
                            nc.tensor.transpose((acc[1][1], tr[0])[b][:, k * P:(k + 1) * P], s_[:, k * P:(k + 1) * P], ident[:, :])
                    for tb in range(TB):
                        mm = nc.tensor.transpose(aux[1][0:NC, tb * P:(tb + 1) * P], self.cs[:, tb, u, 0:NC], ident[:, :])
                    mm.then_inc(PE.sem, PE.one(("PT", u)))
                    if u:
                        self.values_pe(pe, u - 1)
                self.values_pe(pe, 7)

            def values_pe(self, pe, u):
                PE, AC, DV = self.PE, self.AC, self.DV
                g, c = u // 4, u % 4
                pe.wait_ge(AC.sem, AC.at["PT", u])
                if u == 0:
                    pe.wait_ge(DV.sem, DV.at["csm", 1])
                r = slice(64 * g, 64 * g + 64)
                bank = (tr[1], aux[0])[c // 2]
                for tb in range(TB):
                    o = bank[r, (c % 2) * SEQ + tb * P:(c % 2) * SEQ + (tb + 1) * P]
                    ops = [(self.vc[0:NC, r], self.PTc[u % 2][0:NC, tb * P:(tb + 1) * P])]
                    for b in range(2):
                        for k in range(tb + 1):
                            ops.append((self.vt_[:, b, k, r], self.PT[u % 2][b][:, (tb + k) * P:(tb + k + 1) * P]))
                    for i, (a, b_) in enumerate(ops):
                        mm = nc.tensor.matmul(o, a, b_, start=(i == 0), stop=(i == len(ops) - 1))
                mm.then_inc(PE.sem, PE.one(("pv", u)))

            def scores_pe(self, pe, u):
                g, c = u // 4, u % 4
                r = slice(64 * g, 64 * g + 64)
                if u:
                    pe.wait_ge(self.DV.sem, self.DV.at["sm", u - 1, 1])
                else:
                    pe.wait_ge(tr_free[self.uk % 2], self.uk // 2 + 1)
                for b in range(2):
                    bank = (acc[0][1], acc[1][0])[b]
                    nc.tensor.matmul(bank[:, 0:P], self.qf[r, c, 0:P], self.kf[r, b, 0:P], start=True, stop=True)
                    mm = nc.tensor.matmul(bank[:, P:3 * P], self.qf[r, c, P:2 * P], self.kf[r, b, :], start=True, stop=True)
                mm.then_inc(self.PE.sem, self.PE.one(("sc", u)))

            def exps(self, act, u):
                AC, DV = self.AC, self.DV
                for b in range(2):
                    for tb in range(TB):
                        act.wait_ge(DV.sem, DV.at["nm", u, b, tb])
                        o = self.S[u % 2][b][:, 0:P] if tb == 0 else self.S[u % 2][b][:, P:3 * P]
                        i = 2 * b + tb
                        nc.scalar.activation(o, o, ACT.Exp, bias=self.nm[:, u % 2, i:i + 1],
                                                    accum_out=self.sm[:, u % 2, i:i + 1]).then_inc(AC.sem, AC.one(("ex", u, b, tb)))

            def nsa_act(self, act):
                PE, AC, DV, PL = self.PE, self.AC, self.DV, self.PL
                act.wait_ge(PE.sem, PE.at["hid"])
                nc.scalar.activation(self.hs[:, :, 0:NC], aux[0][:, 0:32].rearrange("p (c n) -> p c n", c=2)[:, :, 0:NC], ACT.Silu).then_inc(AC.sem, AC.one("hs"))
                act.wait_ge(PE.sem, PE.at["kvc"])
                nc.scalar.activation(self.kcs[:, 0:NC], aux[1][:, 0:NC], ACT.Copy).then_inc(AC.sem, AC.one("kcs"))
                nc.scalar.activation(self.kcq[:, 0:NC], aux[1][:, 0:NC], ACT.Square).then_inc(AC.sem, AC.one("kcq"))
                nc.scalar.activation(self.vc[0:NC, :], aux[1][0:NC, P:2 * P], ACT.Copy).then_inc(AC.sem, AC.one("vc"))
                self.exps(act, 0)
                act.wait_ge(DV.sem, DV.at["csub"])
                nc.scalar.activation(self.cs[:, :, :, 0:NC], self.cs[:, :, :, 0:NC], ACT.Exp).then_inc(AC.sem, AC.one("cexp"))
                for u in range(8):
                    if u < 7:
                        self.exps(act, u + 1)
                    act.wait_ge(PE.sem, PE.at["PT", u])
                    if u >= 2:
                        act.wait_ge(PE.sem, PE.at["pv", u - 2])
                    for b in range(2):
                        nc.scalar.activation(self.PT[u % 2][b][:, :], (acc[1][1], tr[0])[b][:, 0:384], ACT.Copy).then_inc(AC.sem, AC.one(("PTb", u, b)))
                    nc.scalar.activation(self.PTc[u % 2][0:NC, :], aux[1][0:NC, 0:256], ACT.Copy).then_inc(AC.sem, AC.one(("PT", u)))
                act.wait_ge(PE.sem, PE.at["pv", 7])
                for h in range(2):
                    nc.scalar.activation(self.on[:, 2 * h:2 * h + 2, :].rearrange("p c t -> p (c t)"), (tr[1], aux[0])[h][:, :],
                                                ACT.Copy).then_inc(AC.sem, AC.one(("on", h)))

            def masked(self, dve, u):
                PE, DV = self.PE, self.DV
                dve.wait_ge(PE.sem, PE.at["sc", u])
                if u >= 2:
                    dve.wait_ge(PE.sem, PE.at["PT", u - 2])
                for b in range(2):
                    s_ = self.S[u % 2][b]
                    nc.vector.tensor_tensor(s_[:, :], (acc[0][1], acc[1][0])[b][:, 0:384], self.cneg[:, :], ALU.add).then_inc(DV.sem, DV.one(("sm", u, b)))
                for b in range(2):
                    s_ = self.S[u % 2][b]
                    dve.wait_ge(DV.sem, DV.at["sm", u, b])
                    for tb in range(TB):
                        i = 2 * b + tb
                        nc.vector.tensor_reduce(self.nm[:, u % 2, i:i + 1], s_[:, 0:P] if tb == 0 else s_[:, P:3 * P], AX.X, ALU.max,
                                                       negate=True).then_inc(DV.sem, DV.one(("nm", u, b, tb)))

            def nsa_dve(self, dve):
                PE, AC, DV, PL = self.PE, self.AC, self.DV, self.PL
                dve.wait_ge(PE.sem, PE.at["kcss"])
                dve.wait_ge(PL.sem, PL.at["masks"])
                nc.vector.tensor_scalar(self.krn[:, 0:NC], aux[0][:, 64:64 + NC], 1.0 / ND, EPS, ALU.mult, ALU.add).then_inc(DV.sem, DV.one("kcms"))
                dve.wait_ge(PL.sem, PL.at["kcrn"])
                nc.vector.scalar_tensor_tensor(self.kcf[:, 0:NC], self.kcs[:, 0:NC], vcol("qk_gain", 1), self.krn[:, 0:NC],
                                                      ALU.mult, ALU.mult).then_inc(DV.sem, DV.one("kcf"))
                self.masked(dve, 0)
                dve.wait_ge(PE.sem, PE.at["csc"])
                m = [P, TB, 4, NC]
                for g in range(2):
                    nc.vector.tensor_tensor(self.cs[:, :, 4 * g:4 * g + 4, 0:NC],
                                                   (acc[0][0], aux[0])[g][:, 0:128].rearrange("p (t c n) -> p t c n", t=TB, c=4)[:, :, :, 0:NC],
                                                   self.cmask[:, :, 0:NC].unsqueeze(2).broadcast_to(m), ALU.add).then_inc(DV.sem, DV.one(("csm", g)))
                dve.wait_ge(DV.sem, DV.at["csm", 1])
                cs = self.cs[:, :, :, 0:NC]
                m = [P, TB, NH, NC]
                nc.vector.tensor_reduce(self.cm[:, :, :], cs, AX.X, ALU.max).then_inc(DV.sem, DV.one("cmax"))
                dve.wait_ge(DV.sem, DV.at["cmax"])
                nc.vector.tensor_tensor(cs, cs, self.cm[:, :, :].unsqueeze(3).broadcast_to(m), ALU.subtract).then_inc(DV.sem, DV.one("csub"))
                dve.wait_ge(AC.sem, AC.at["cexp"])
                nc.vector.tensor_reduce(self.csum[:, :, :], cs, AX.X, ALU.add).then_inc(DV.sem, DV.one("csum"))
                nc.vector.tensor_tensor(cs, cs, self.cm01[:, :, 0:NC].unsqueeze(2).broadcast_to(m), ALU.mult).then_inc(DV.sem, DV.one("c01"))
                dve.wait_ge(PL.sem, PL.at["cinv"])
                gates = self.gt[:, :, :].rearrange("p t (h k) -> p t h k", k=3)
                nc.vector.tensor_tensor(self.ccoef[:, :, :], self.ccoef[:, :, :], gates[:, :, :, 0], ALU.mult).then_inc(DV.sem, DV.one("ccoef"))
                dve.wait_ge(DV.sem, DV.at["ccoef"])
                nc.vector.tensor_tensor(cs, cs, self.ccoef[:, :, :].unsqueeze(3).broadcast_to(m), ALU.mult).then_inc(DV.sem, DV.one("Pc"))
                for u in range(8):
                    if u < 7:
                        self.masked(dve, u + 1)
                    dve.wait_ge(AC.sem, AC.at["ex", u, 1, 1])
                    nc.vector.reciprocal(self.inv_[:, u % 2, :], self.sm[:, u % 2, :]).then_inc(DV.sem, DV.one(("inv", u)))
                    dve.wait_ge(DV.sem, DV.at["inv", u])
                    nc.vector.tensor_tensor(self.coef[:, u % 2, :].rearrange("p (b t) -> p b t", b=2),
                                                   self.inv_[:, u % 2, :].rearrange("p (b t) -> p b t", b=2),
                                                   gates[:, :, u, 1:3].rearrange("p t b -> p b t"), ALU.mult).then_inc(DV.sem, DV.one(("coef", u)))
                    dve.wait_ge(DV.sem, DV.at["coef", u])
                    for b in range(2):
                        for tb in range(TB):
                            i = 2 * b + tb
                            o = self.S[u % 2][b][:, 0:P] if tb == 0 else self.S[u % 2][b][:, P:3 * P]
                            nc.vector.tensor_scalar(o, o, self.coef[:, u % 2, i:i + 1], None, ALU.mult).then_inc(DV.sem, DV.one(("P", u, b, tb) if i < 3 else ("P", u)))

            def nsa_pool(self, pool):
                PE, AC, DV, PL = self.PE, self.AC, self.DV, self.PL
                pool.wait_ge(DV.sem, DV.at["kcms"])
                nc.gpsimd.tensor_tensor(self.krn[:, 0:NC], self.krn[:, 0:NC], mhalf[:, 0:NC], ALU.pow).then_inc(PL.sem, PL.one("kcrn"))
                pool.wait_ge(DV.sem, DV.at["csum"])
                nc.gpsimd.tensor_tensor(self.ccoef[:, :, :], self.csum[:, :, :], minus1[:, 0:16].rearrange("p (t h) -> p t h", t=TB),
                                               ALU.pow).then_inc(PL.sem, PL.one("cinv"))

            def rwkv_pe(self, pe):
                PE, AC, DV, PL = self.PE, self.AC, self.DV, self.PL
                pe.wait_ge(AC.sem, AC.at["on", 1])
                pe.wait_ge(AC.sem, AC.at["sgd"])
                b4 = (acc[0][0], acc[0][1]), (acc[1][0], acc[1][1]), (tr[0], tr[1])
                for i, (w, x, r) in enumerate(((self.wua, 12, slice(0, 64)), (self.wua, 12, slice(64, 128)), (self.gup, 13, slice(0, 128)))):
                    for p in range(4):
                        mm = nc.tensor.matmul(b4[i][p // 2][:, (p % 2) * SEQ:(p % 2 + 1) * SEQ], w[r, p * P:(p + 1) * P], self.rwf[r, x, :],
                                              start=True, stop=True)
                    mm.then_inc(PE.sem, PE.one(("low_rank", i)))
                pe.wait_ge(AC.sem, AC.at["kksq"])
                for tb in range(TB):
                    for p in range(4):
                        mm = nc.tensor.matmul(aux[0][:, (tb * 4 + p) * 2:(tb * 4 + p) * 2 + 2], self.tmp[7][:, p, tb * P:(tb + 1) * P],
                                              self.blk[:, 0:P:64], start=True, stop=True)
                mm.then_inc(PE.sem, PE.one("kss"))
                pe.wait_ge(DV.sem, DV.at["krnx"])
                for p in range(4):
                    for tb in range(TB):
                        mm = nc.tensor.matmul(b4[0][p // 2][:, (p % 2) * SEQ + tb * P:(p % 2) * SEQ + (tb + 1) * P],
                                              self.tmp[2][:, :, :].rearrange("p a t -> p (a t)")[:, (tb * 4 + p) * P:(tb * 4 + p + 1) * P],
                                              ident[:, :], start=True, stop=True)
                mm.then_inc(PE.sem, PE.one("krb"))
                pe.wait_ge(DV.sem, DV.at["rk", 3])
                for p in range(4):
                    mm = nc.tensor.matmul(b4[1][p // 2][:, (p % 2) * SEQ:(p % 2 + 1) * SEQ], self.blk[:, :], self.tmp[0][:, p, :], start=True, stop=True)
                mm.then_inc(PE.sem, PE.one("bon"))
                banks = [tr[0], tr[1], aux[0], aux[1], acc[0][0], acc[0][1]]
                pe.wait_ge(AC.sem, AC.at["g", 1])
                for i, src in enumerate((self.rwf[:, 8:12, :], self.be, self.ka)):
                    if i == 0:
                        pe.wait_ge(AC.sem, AC.at["shift", 13])
                    if i == 1:
                        pe.wait_ge(PL.sem, PL.at["be"])
                    if i == 2:
                        pe.wait_ge(PL.sem, PL.at["ka"])
                        pe.wait_ge(DV.sem, DV.at["kkn", 1])
                    for tb in range(TB):
                        for p in range(4):
                            mm = nc.tensor.transpose(banks[2 * i + tb][:, p * P:(p + 1) * P], src[:, p, tb * P:(tb + 1) * P], ident[:, :])
                        mm.then_inc(PE.sem, PE.one(("tm", i, tb)))
                pe.wait_ge(PL.sem, PL.at["rt"])
                pe.wait_ge(PL.sem, PL.at["al"])
                pe.wait_ge(DV.sem, DV.at["bonus", 1])
                pe.wait_ge(AC.sem, AC.at["tm", 2, 1])
                for Bt in range(2):
                    self.core_pe(pe, Bt)
                pe.wait_ge(DV.sem, DV.at["yn"])
                for p in range(4):
                    for tb in range(TB):
                        mm = nc.tensor.transpose((tr[0], tr[1])[p // 2][:, (p % 2) * SEQ + tb * P:(p % 2) * SEQ + (tb + 1) * P],
                                                 self.y[:, tb, 2 * p:2 * p + 2, :].rearrange("p h d -> p (h d)"), ident[:, :])
                mm.then_inc(PE.sem, PE.one("yt"))
                pe.wait_ge(AC.sem, AC.at["yf", 3])

            def unit(self, j):
                return j // 4, j // 2 % 2, j % 2

            def core_pe(self, pe, Bt):
                PE, AC, DV, PL = self.PE, self.AC, self.DV, self.PL
                if Bt:
                    pe.wait_ge(DV.sem, DV.at["yb", Bt - 1, 1])
                for j in range(8):
                    q, hp, tb = self.unit(j)
                    r = slice(64 * hp, 64 * hp + 64)
                    p = 2 * Bt + q
                    t = slice(tb * P, (tb + 1) * P)
                    i = hp
                    o = slice((2 * q + tb) * P, (2 * q + tb + 1) * P)
                    al, rt, be, ka = (x[r, p, t] for x in (self.al, self.rt, self.be, self.ka))
                    nc.tensor.matmul((acc[0][0], acc[0][1])[i][:, o], al, be, start=True, stop=True)
                    nc.tensor.matmul((acc[1][0], acc[1][1])[i][:, o], ka, al, start=True, stop=True)
                    nc.tensor.matmul((tr[0], tr[1])[i][:, o], ka, rt, start=True, stop=True)
                    mm = nc.tensor.matmul((aux[0], aux[1])[i][:, o], be, rt, start=True, stop=True)
                mm.then_inc(PE.sem, PE.one(("gram", Bt)))
                pe.wait_ge(AC.sem, AC.at["A", Bt, 1])
                pe.wait_ge(DV.sem, DV.at["RB", Bt, 1])
                self.inv.pe(pe, Bt)
                pe.wait_ge(self.inv.u_ready, 12 * (Bt + 1))
                for j in range(8):
                    q, hp, tb = self.unit(j)
                    h = 2 * q + hp
                    mm = nc.tensor.matmul(acc[1][0][:, (tb * 4 + h) * ND:(tb * 4 + h + 1) * ND], self.G1[:, j, :],
                                          self.vt[:, tb, (4 * Bt + h) * ND:(4 * Bt + h + 1) * ND], start=True, stop=True)
                mm.then_inc(PE.sem, PE.one(("gv", Bt)))
                for c in range(4):
                    tb, hf = c // 2, c % 2
                    rows = slice(64 * hf, 64 * hf + 64)
                    for h in range(4):
                        k = (4 * Bt + h) * ND
                        mm = nc.tensor.matmul((tr[0], tr[1])[hf][64 * (h % 2):64 * (h % 2) + 64, (tb * 2 + h // 2) * ND:(tb * 2 + h // 2 + 1) * ND],
                                              self.kt[rows, tb, k:k + ND], self.vt[rows, tb, k:k + ND], start=True, stop=True)
                mm.then_inc(PE.sem, PE.one(("kv", Bt)))
                keep_clock(pe, 4, acc[0][1])
                for c in range(4):
                    tb, hf = c // 2, c % 2
                    rows = slice(64 * hf, 64 * hf + 64)
                    tt = slice(64 * c, 64 * c + 64)
                    if c:
                        keep_clock(pe, 3, tr[1])
                        pe.wait_ge(DV.sem, DV.at["M", Bt, c - 1])
                        pe.wait_ge(AC.sem, AC.at["RM", Bt, c - 1]) if c > 1 else None
                        for h in range(4):
                            p, hp = h // 2, h % 2
                            r = slice(64 * hp, 64 * hp + 64)
                            bank = (acc[1][1], aux[1])[hp]
                            nc.tensor.matmul(bank[rows, p * ND:(p + 1) * ND], self.al[r, 2 * Bt + p, tt], self.M[r, p, :], start=True, stop=True)
                            mm = nc.tensor.matmul(bank[rows, (2 + p) * ND:(3 + p) * ND], self.rt[r, 2 * Bt + p, tt], self.M[r, p, :], start=True, stop=True)
                        mm.then_inc(PE.sem, PE.one(("aM", Bt, c)))
                    if c:
                        keep_clock(pe, 3, tr[1])
                    pe.wait_ge(DV.sem, DV.at["N1", Bt, c])
                    for h in range(4):
                        j = (h // 2) * 4 + (h % 2) * 2 + tb
                        mm = nc.tensor.matmul(acc[0][0][rows, h * ND:(h + 1) * ND], self.U[rows, j, 64 * hf:64 * hf + 64], self.N1[rows, h, :],
                                              start=True, stop=True)
                    mm.then_inc(PE.sem, PE.one(("TN", Bt, c)))
                    keep_clock(pe, 3, tr[1]) if c else None
                    pe.wait_ge(DV.sem, DV.at["SA", Bt, c])
                    if c < 3:
                        for h in range(4):
                            k = (4 * Bt + h) * ND
                            mm = nc.tensor.matmul(aux[0][64 * (h % 2):64 * (h % 2) + 64, (h // 2) * ND:(h // 2 + 1) * ND], self.bt[rows, tb, k:k + ND],
                                                  self.SA[rows, h, :], start=True, stop=True)
                        mm.then_inc(PE.sem, PE.one(("bSA", Bt, c)))
                    if hf:
                        if tb:
                            pe.wait_ge(DV.sem, DV.at["yb", Bt, 0])
                        for h in range(4):
                            j = (h // 2) * 4 + (h % 2) * 2 + tb
                            k = (4 * Bt + h) * ND
                            o = acc[0][1][:, h * ND:(h + 1) * ND]
                            nc.tensor.matmul(o, self.RB[:, j, :], self.SA[:, h, :], start=True, stop=False)
                            mm = nc.tensor.matmul(o, self.RK[:, j, :], self.vt[:, tb, k:k + ND], start=False, stop=True)
                        mm.then_inc(PE.sem, PE.one(("Y", Bt, tb)))

            def rwkv_act(self, act):
                PE, AC, DV, PL = self.PE, self.AC, self.DV, self.PL
                act.wait_ge(tr_free[(self.ur + 6) % 2], (self.ur + 6) // 2 + 1)
                nc.scalar.activation(self.rwf[0:64, 12, :], self.rwf[0:64, 12, :], ACT.Tanh).then_inc(AC.sem, AC.one("tw"))
                nc.scalar.activation(self.rwf[:, 13, :], self.rwf[:, 13, :], ACT.Sigmoid).then_inc(AC.sem, AC.one("sgd"))
                for i, (dst, b) in enumerate(((self.tmp[0], "w0"), (self.tmp[5], "a0"))):
                    act.wait_ge(PE.sem, PE.at["low_rank", i])
                    for p in range(4):
                        nc.scalar.activation(dst[:, p, :], acc[i][p // 2][:, (p % 2) * SEQ:(p % 2 + 1) * SEQ], ACT.Sigmoid, bias=vcol(b, p)).then_inc(AC.sem, AC.one(("sig", i, p)))
                for p in range(4):
                    nc.scalar.activation(self.tmp[6][:, p, :], self.rwf[:, 4 + p, :], ACT.Copy, scale=vcol("k_k", p)).then_inc(AC.sem, AC.one(("kk", p)))
                act.wait_ge(AC.sem, AC.at["kk", 3])
                nc.scalar.activation(self.tmp[7][:, :, :], self.tmp[6][:, :, :], ACT.Square).then_inc(AC.sem, AC.one("kksq"))
                act.wait_ge(PE.sem, PE.at["low_rank", 2])
                for i in range(2):
                    nc.scalar.activation(self.g[:, 2 * i:2 * i + 2, :].rearrange("p c t -> p (c t)"), (tr[0], tr[1])[i][:, :], ACT.Copy).then_inc(AC.sem, AC.one(("g", i)))
                act.wait_ge(DV.sem, DV.at["cs", 3])
                nc.scalar.activation(self.tmp[4][:, :, :], self.tmp[1][:, :, :], ACT.Exp).then_inc(AC.sem, AC.one("cw"))
                nc.scalar.activation(self.tmp[3][:, :, :], self.tmp[1][:, :, :], ACT.Exp, scale=-1.0).then_inc(AC.sem, AC.one("icw"))
                act.wait_ge(DV.sem, DV.at["csp"])
                nc.scalar.activation(self.al[:, :, :], self.rt[:, :, :], ACT.Exp).then_inc(AC.sem, AC.one("cwp"))
                banks = [tr[0], tr[1], aux[0], aux[1], acc[0][0], acc[0][1]]
                for i, dst in enumerate((self.vt, self.bt, self.kt)):
                    for tb in range(TB):
                        act.wait_ge(PE.sem, PE.at["tm", i, tb])
                        nc.scalar.activation(dst[:, tb, :], banks[2 * i + tb][:, :], ACT.Copy).then_inc(AC.sem, AC.one(("tm", i, tb)))
                for Bt in range(2):
                    act.wait_ge(PE.sem, PE.at["gram", Bt])
                    for i in range(2):
                        o = self.A[:, :, :].rearrange("p (q h t) s -> p q h t s", q=2, h=2)[:, :, i]
                        nc.scalar.activation(o, (acc[0][0], acc[0][1])[i][:, :].rearrange("p (q t s) -> p q t s", q=2, t=2), ACT.Copy).then_inc(AC.sem, AC.one(("A", Bt, i)))
                    self.inv.act(act, Bt)
                    for c in range(1, 4):
                        hf, tb = c % 2, c // 2
                        rows = slice(64 * hf, 64 * hf + 64)
                        act.wait_ge(DV.sem, DV.at["N1", Bt, c])
                        for hp in range(2):
                            if c == 2 and hp == 0:
                                act.wait_ge(DV.sem, DV.at["yb", Bt, 0])
                            if hp == 0 and c != 2:
                                pass
                            x = nc.scalar.activation(self.RM[rows, hp:4:2, :], (acc[1][1], aux[1])[hp][rows, 2 * ND:4 * ND].rearrange("p (q d) -> p q d", q=2),
                                                     ACT.Copy)
                            x.then_inc(AC.sem, AC.one(("RM", Bt, c) if hp else ("RM", Bt, c, 0)))
                act.wait_ge(DV.sem, DV.at["ycen"])
                nc.scalar.activation(self.ysq[:, :, :, :], self.y[:, :, :, :], ACT.Square).then_inc(AC.sem, AC.one("ysq"))
                act.wait_ge(PE.sem, PE.at["yt"])
                for p in range(4):
                    nc.scalar.activation(self.tmp[0][:, p, :], (tr[0], tr[1])[p // 2][:, (p % 2) * SEQ:(p % 2 + 1) * SEQ], ACT.Identity,
                                                scale=vcol("ln_w", p), bias=vcol("ln_b", p)).then_inc(AC.sem, AC.one(("yf", p)))

            def rwkv_dve(self, dve):
                PE, AC, DV, PL = self.PE, self.AC, self.DV, self.PL
                f = float(np.exp(-0.5))
                dve.wait_ge(AC.sem, AC.at["sig", 0, 3])
                nc.vector.tensor_scalar(self.tmp[0][:, :, :], self.tmp[0][:, :, :], -f, None, ALU.mult).then_inc(DV.sem, DV.one("lw"))
                dve.wait_ge(DV.sem, DV.at["lw"])
                for p in range(4):
                    nc.vector.tensor_tensor_scan(self.tmp[1][:, p, :], self.fresh[:, :], self.tmp[0][:, p, :], 0.0, ALU.mult, ALU.add).then_inc(DV.sem, DV.one(("cs", p)))
                dve.wait_ge(DV.sem, DV.at["cs", 3])
                nc.vector.tensor_tensor(self.rt[:, :, :], self.tmp[1][:, :, :], self.tmp[0][:, :, :], ALU.subtract).then_inc(DV.sem, DV.one("csp"))
                dve.wait_ge(PE.sem, PE.at["kss"])
                nc.vector.tensor_scalar(self.rinv[:, :], aux[0][:, 0:16], 1e-24, None, ALU.max).then_inc(DV.sem, DV.one("kmx"))
                dve.wait_ge(PL.sem, PL.at["kkrn"])
                nc.vector.tensor_copy(self.tmp[2][:, :, :].rearrange("p a t -> p (a t)").rearrange("p (n d) -> p n d", d=ND),
                                             self.rinv[:, :].unsqueeze(2).broadcast_to([P, 16, ND])).then_inc(DV.sem, DV.one("krnx"))
                dve.wait_ge(PE.sem, PE.at["krb"])
                for i in range(2):
                    o = self.tmp[6][:, 2 * i:2 * i + 2, :].rearrange("p c t -> p (c t)")
                    nc.vector.tensor_tensor(o, o, acc[0][i][:, :], ALU.mult).then_inc(DV.sem, DV.one(("kkn", i)))
                dve.wait_ge(DV.sem, DV.at["kkn", 1])
                dve.wait_ge(AC.sem, AC.at["sig", 1, 3])
                nc.vector.tensor_tensor(self.tmp[7][:, :, :], self.tmp[6][:, :, :], self.tmp[5][:, :, :], ALU.mult).then_inc(DV.sem, DV.one("bb"))
                dve.wait_ge(DV.sem, DV.at["bb"])
                for p in range(4):
                    nc.vector.tensor_scalar(self.tmp[5][:, p, :], self.tmp[5][:, p, :], -1.0, vcol("k_a", p), ALU.add, ALU.mult).then_inc(DV.sem, DV.one(("ka1", p)))
                dve.wait_ge(DV.sem, DV.at["ka1", 3])
                k = self.rwf[:, 4:8, :].rearrange("p c t -> p (c t)")
                nc.vector.scalar_tensor_tensor(k, self.tmp[5][:, :, :].rearrange("p c t -> p (c t)"), 1.0, k, ALU.add, ALU.mult).then_inc(DV.sem, DV.one("kp"))
                dve.wait_ge(DV.sem, DV.at["kp"])
                for p in range(4):
                    nc.vector.scalar_tensor_tensor(self.tmp[0][:, p, :], self.rwf[:, p, :], vcol("r_k", p), self.rwf[:, 4 + p, :],
                                                          ALU.mult, ALU.mult).then_inc(DV.sem, DV.one(("rk", p)))
                dve.wait_ge(AC.sem, AC.at["cw"])
                nc.vector.tensor_copy(self.cwl[:, :, :], self.tmp[4][:, :, 63:SEQ:64]).then_inc(DV.sem, DV.one("cwl"))
                dve.wait_ge(PE.sem, PE.at["bon"])
                for i in range(2):
                    nc.vector.tensor_tensor(self.bonus[:, 2 * i:2 * i + 2, :].rearrange("p c t -> p (c t)"), acc[1][i][:, :],
                                                   self.rwf[:, 8 + 2 * i:10 + 2 * i, :].rearrange("p c t -> p (c t)"), ALU.mult).then_inc(DV.sem, DV.one(("bonus", i)))
                for Bt in range(2):
                    dve.wait_ge(PE.sem, PE.at["gram", Bt])
                    if Bt == 0:
                        dve.wait_ge(PL.sem, PL.at["tmp_free"])
                    for dst, banks, mask, name in ((self.G1, (acc[1][0], acc[1][1]), self.st64, "G1"), (self.RK, (tr[0], tr[1]), self.i64, "RK"),
                                                   (self.RB, (aux[0], aux[1]), self.i64, "RB")):
                        for i in range(2):
                            o = dst[:, :, :].rearrange("p (q h t) s -> p q h t s", q=2, h=2)[:, :, i]
                            nc.vector.tensor_tensor(o, banks[i][:, :].rearrange("p (q t s) -> p q t s", q=2, t=2),
                                                           mask[:, :].unsqueeze(1).unsqueeze(1).broadcast_to([P, 2, 2, P]), ALU.mult).then_inc(DV.sem, DV.one((name, Bt, i)))
                    self.inv.dve(dve, Bt)
                    dve.wait_ge(PE.sem, PE.at["gv", Bt])
                    nc.vector.tensor_copy(self.gv[:, :, :, :].rearrange("p t h d -> p (t h d)"), acc[1][0][:, :]).then_inc(DV.sem, DV.one(("gv", Bt)))
                    dve.wait_ge(PE.sem, PE.at["kv", Bt])
                    for hf in range(2):
                        nc.vector.tensor_copy(self.kvs[:, hf:4:2].rearrange("p c q d -> p c (q d)"),
                                                     (tr[0], tr[1])[hf][:, 0:256].rearrange("p (c q) -> p c q", c=2)).then_inc(DV.sem, DV.one(("kv", Bt, hf)))
                    dve.wait_ge(DV.sem, DV.at["kv", Bt, 1])
                    for c in range(4):
                        tb, hf = c // 2, c % 2
                        rows = slice(64 * hf, 64 * hf + 64)
                        if c == 0:
                            nc.vector.tensor_copy(self.N1[rows], self.gv[rows, tb]).then_inc(DV.sem, DV.one(("N1", Bt, c)))
                        else:
                            dve.wait_ge(PE.sem, PE.at["aM", Bt, c])
                            for hp in range(2):
                                x = nc.vector.tensor_tensor(self.N1[rows, hp:4:2, :], (acc[1][1], aux[1])[hp][rows, 0:2 * ND].rearrange("p (q d) -> p q d", q=2),
                                                            self.gv[rows, tb, hp:4:2, :], ALU.add)
                                x.then_inc(DV.sem, DV.one(("N1", Bt, c) if hp else ("N1", Bt, c, 0)))
                        dve.wait_ge(PE.sem, PE.at["TN", Bt, c])
                        if c == 2:
                            dve.wait_ge(PE.sem, PE.at["Y", Bt, 0])
                        nc.vector.tensor_scalar(self.SA[rows].rearrange("p h d -> p (h d)"), acc[0][0][rows, 0:256], -1.0, None, ALU.mult).then_inc(DV.sem, DV.one(("SA", Bt, c)))
                        if c < 3:
                            m = self.M[:, :, :]
                            if c:
                                nc.vector.tensor_tensor(m, m, self.kvs[:, c], ALU.add).then_inc(DV.sem, DV.one(("M1", Bt, c)))
                                dve.wait_ge(DV.sem, DV.at["M1", Bt, c])
                            dve.wait_ge(PE.sem, PE.at["bSA", Bt, c])
                            nc.vector.tensor_tensor(m, aux[0][:, 0:2 * ND].rearrange("p (q d) -> p q d", q=2), m if c else self.kvs[:, c], ALU.add).then_inc(DV.sem, DV.one(("M2", Bt, c)))
                            dve.wait_ge(DV.sem, DV.at["M2", Bt, c])
                            nc.vector.tensor_tensor(m, m, self.cwl[:, 2 * Bt:2 * Bt + 2, c:c + 1].broadcast_to([P, 2, ND]), ALU.mult).then_inc(DV.sem, DV.one(("M", Bt, c)))
                        if hf:
                            dve.wait_ge(PE.sem, PE.at["Y", Bt, tb])
                            y = self.y[:, tb, 4 * Bt:4 * Bt + 4, :]
                            if tb == 0:
                                dve.wait_ge(AC.sem, AC.at["RM", Bt, 1])
                                nc.vector.tensor_copy(y[0:64], acc[0][1][0:64, 0:256].rearrange("p (h d) -> p h d", h=4)).then_inc(DV.sem, DV.one(("yb0", Bt)))
                                nc.vector.tensor_tensor(y[64:128], acc[0][1][64:128, 0:256].rearrange("p (h d) -> p h d", h=4),
                                                               self.RM[64:128], ALU.add).then_inc(DV.sem, DV.one(("yb", Bt, tb)))
                            else:
                                dve.wait_ge(AC.sem, AC.at["RM", Bt, 3])
                                nc.vector.tensor_tensor(y, acc[0][1][:, 0:256].rearrange("p (h d) -> p h d", h=4), self.RM[:, :, :], ALU.add).then_inc(DV.sem, DV.one(("yb", Bt, tb)))
                y = self.y[:, :, :, :]
                st = self.ln
                mean, var = st[:, 0:16].rearrange("p (t h) -> p t h", t=TB), st[:, 16:32].rearrange("p (t h) -> p t h", t=TB)
                full = [P, TB, NH, ND]
                dve.wait_ge(DV.sem, DV.at["yb", 1, 1])
                nc.vector.tensor_reduce(mean, y, AX.X, ALU.add).then_inc(DV.sem, DV.one("ysum"))
                dve.wait_ge(DV.sem, DV.at["ysum"])
                nc.vector.tensor_scalar(mean, mean, 1.0 / ND, None, ALU.mult).then_inc(DV.sem, DV.one("ymean"))
                dve.wait_ge(DV.sem, DV.at["ymean"])
                nc.vector.tensor_tensor(y, y, mean.unsqueeze(3).broadcast_to(full), ALU.subtract).then_inc(DV.sem, DV.one("ycen"))
                dve.wait_ge(AC.sem, AC.at["ysq"])
                nc.vector.tensor_reduce(var, self.ysq[:, :, :, :], AX.X, ALU.add).then_inc(DV.sem, DV.one("ysqs"))
                dve.wait_ge(DV.sem, DV.at["ysqs"])
                nc.vector.tensor_scalar(var, var, 1.0 / ND, 1e-5 * ND, ALU.mult, ALU.add).then_inc(DV.sem, DV.one("yvar"))
                dve.wait_ge(PL.sem, PL.at["yrn"])
                rn = st[:, 32:48].rearrange("p (t h) -> p t h", t=TB)
                nc.vector.tensor_tensor(y, y, rn.unsqueeze(3).broadcast_to(full), ALU.mult).then_inc(DV.sem, DV.one("yn"))
                dve.wait_ge(AC.sem, AC.at["yf", 3])
                o = self.tmp[0][:, :, :]
                nc.vector.tensor_tensor(o, o, self.bonus[:, :, :], ALU.add).then_inc(DV.sem, DV.one("ybon"))

            def rwkv_pool(self, pool):
                PE, AC, DV, PL = self.PE, self.AC, self.DV, self.PL
                m = nc.gpsimd
                pool.wait_ge(DV.sem, DV.at["kmx"])
                m.tensor_tensor(self.rinv[:, :], self.rinv[:, :], mhalf[:, 0:16], ALU.pow).then_inc(PL.sem, PL.one("kkrn"))
                pool.wait_ge(AC.sem, AC.at["cwp"])
                pool.wait_ge(AC.sem, AC.at["cw"])
                pool.wait_ge(DV.sem, DV.at["kkn", 1])
                m.tensor_tensor(self.al[:, :, :], self.al[:, :, :], self.tmp[6][:, :, :], ALU.mult).then_inc(PL.sem, PL.one("al"))
                m.tensor_tensor(self.rt[:, :, :], self.rwf[:, 0:4, :], self.tmp[4][:, :, :], ALU.mult).then_inc(PL.sem, PL.one("rt"))
                pool.wait_ge(DV.sem, DV.at["bb"])
                pool.wait_ge(AC.sem, AC.at["icw"])
                m.tensor_tensor(self.be[:, :, :], self.tmp[7][:, :, :], self.tmp[3][:, :, :], ALU.mult).then_inc(PL.sem, PL.one("be"))
                pool.wait_ge(DV.sem, DV.at["kp"])
                m.tensor_tensor(self.ka[:, :, :], self.rwf[:, 4:8, :], self.tmp[3][:, :, :], ALU.mult).then_inc(PL.sem, PL.one("ka"))
                pool.wait_ge(PE.sem, PE.at["bon"])
                pool.wait_ge(PE.sem, PE.at["krb"])
                pool.wait_ge(DV.sem, DV.at["cwl"])
                pool.wait_ge(PL.sem, PL.at["ka"])
                m.memset(self.RM[:, :, :], 0.0).then_inc(PL.sem, PL.one("tmp_free"))
                for Bt in range(2):
                    self.inv.used = None
                    if Bt:
                        pool.wait_ge(DV.sem, DV.at["yb", 0, 1])
                    else:
                        pool.wait_ge(PL.sem, PL.at["tmp_free"])
                    self.inv.pool(pool, Bt)
                pool.wait_ge(DV.sem, DV.at["yvar"])
                m.tensor_tensor(self.ln[:, 32:48], self.ln[:, 16:32], mhalf[:, 0:16], ALU.pow).then_inc(PL.sem, PL.one("yrn"))
                pool.wait_ge(DV.sem, DV.at["ybon"])
                m.tensor_tensor(self.rwf[:, 8:12, :], self.tmp[0][:, :, :], self.g[:, :, :], ALU.mult).then_inc(PL.sem, PL.one("or"))

        def add_act(act, gi):
            for c in range(2):
                if c == 0:
                    stream_act(act, gi)
                for tb in range(TB):
                    act.wait_ge(acc_ready, 2 * (gi + c) + tb + 1)
                    nc.scalar.activation(work[:, tb, c * GW:(c + 1) * GW], acc[(gi + c) % 2][tb][:, :],
                                         ACT.Copy).then_inc(acc_free[(gi + c) % 2][tb], 1)
                if c == 0:
                    stream_act(act, gi + 1)

        def add_dve(dve, gi):
            for tb in range(TB):
                add_branch(dve, gi, tb)

        class ConvFfn:
            def __init__(self):
                self.up, self.down = first["ffn2_up"], first["ffn2_down"]
                self.n, self.post = plan["pre"], plan["post"]
                self.norm_unit = plan["unit"]
                self.unit = plan["unit"] + DC // 2
                plan["pre"] += 1
                plan["post"] += 1
                plan["unit"] += DC // 2 + 2 * FG
                self.g0 = lambda c: vcol("norm_ffn", c)
                self.tap2, self.tap1, self.half, self.silu_done, self.y_done, self.high_done, self.low_done = (
                    sem("ffn2_" + x) for x in ("tap2", "tap1", "half", "silu", "y", "high", "low"))
                c = Carve(arena_at, 10 * 4096)
                self.conv = [[c(f"ffn2_conv{i}{h}", [2, SEQ]) for h in range(2)] for i in range(2)]
                self.y = [c(f"ffn2_y{i}", [2 * SEQ]) for i in range(2)]

            def sp(self, sp):
                for t in group_tiles(self.up):
                    load(sp, t)
                t0 = tile_of[self.up + 1]
                for t in range(t0, t0 + 4):
                    load(sp, t)
                with sp.Fori(1, LOOPS) as i:
                    for t in range(t0, t0 + 4):
                        load(sp, t, i, 512)
                for gi in (self.down, self.down + 1):
                    for t in group_tiles(gi):
                        load(sp, t)

            def turn_pe(self, pe, g, i=0):
                gi = self.up + g
                for tb in range(TB):
                    pe.wait_ge(acc_free[gi % 2][tb], gi // 2 + 1 + i)
                for h in range(2):
                    u = self.unit + 2 * g + h
                    pe.wait_ge(tr_free[u % 2], u // 2 + 2 * i)
                    for c in range(2):
                        for tb in range(TB):
                            mm = nc.tensor.transpose(tr[u % 2][:, c * SEQ + tb * P:c * SEQ + (tb + 1) * P],
                                                     prod[gi % 2][tb][:, (2 * h + c) * P:(2 * h + c + 1) * P], ident[:, :])
                    mm.then_inc(tr_ready, 1)

            def to_prod(self, act, g, i=0):
                gi = self.up + g
                for tb in range(TB):
                    act.wait_ge(acc_ready, 2 * gi + tb + 1 + 4 * i)
                    nc.scalar.activation(prod[gi % 2][tb][:, :], acc[gi % 2][tb][:, :], ACT.Copy).then_inc(acc_free[gi % 2][tb], 1)

            def weight(self, tap, h, g, c, i):
                return vcol("ffn_conv", i * 4 + (tap * 2 * FC + h * FC + 2 * g + c))

            def tap2_act(self, act, g, i=0):
                act.wait_ge(self.y_done, g - 1 + 2 * i) if g > 1 or not isinstance(i, int) else None
                for h in range(2):
                    u = self.unit + 2 * g + h
                    act.wait_ge(tr_ready, u + 1 + 4 * i)
                    for c in range(2):
                        nc.scalar.activation(self.conv[g % 2][h][:, c, :], tr[u % 2][:, c * SEQ:(c + 1) * SEQ], ACT.Copy,
                                             scale=self.weight(2, h, g, c, i)).then_inc(self.tap2, 1)

            def taps_dve(self, dve, g, i=0):
                for h in range(2):
                    u = self.unit + 2 * g + h
                    dve.wait_ge(self.tap2, 4 * g + 2 * h + 2 + 8 * i)
                    for tap in (1, 0):
                        for c in range(2):
                            d = 2 - tap
                            o = self.conv[g % 2][h][:, c, d:]
                            if tap == 0:
                                dve.wait_ge(self.tap1, 4 * g + 2 * h + c + 1 + 8 * i)
                            x = nc.vector.scalar_tensor_tensor(o, tr[u % 2][:, c * SEQ:(c + 1) * SEQ - d], self.weight(tap, h, g, c, i), o,
                                                               ALU.mult, ALU.add)
                            x.then_inc(self.tap1 if tap else (tr_free[u % 2] if c else self.half), 1)

            def silu_act(self, act, g, i=0):
                u = self.unit + 2 * g
                act.wait_ge(tr_free[u % 2], u // 2 + 1 + 2 * i)
                a = self.conv[g % 2][0]
                nc.scalar.activation(a[:, :, :], a[:, :, :], ACT.Silu).then_inc(self.silu_done, 1)

            def y_pool(self, pool, g, i=0):
                u = self.unit + 2 * g + 1
                pool.wait_ge(self.silu_done, g + 1 + 2 * i)
                pool.wait_ge(tr_free[u % 2], u // 2 + 1 + 2 * i)
                a, b = self.conv[g % 2]
                nc.gpsimd.tensor_tensor(self.y[g % 2][:, :], a[:, :, :].rearrange("p c t -> p (c t)"), b[:, :, :].rearrange("p c t -> p (c t)"),
                                        ALU.mult).then_inc(self.y_done, 1)

            def place(self, x, g, i):
                x = x[:, :, :].rearrange("p c t -> p (c t)")
                return x[:, g * 512:(g + 1) * 512] if isinstance(i, int) else x[:, bass.ds(i * 1024 + g * 512, 512)]

            def high_act(self, act, g, i=0):
                act.wait_ge(self.y_done, g + 1 + 2 * i)
                nc.scalar.activation(self.place(hh, g, i), self.y[g % 2][:, :], ACT.Copy).then_inc(self.high_done, 1)

            def low_pool(self, pool, g, i=0):
                pool.wait_ge(self.high_done, g + 1 + 2 * i)
                nc.gpsimd.tensor_tensor(self.place(hl, g, i), self.y[g % 2][:, :], self.place(hh, g, i).bitcast(F32),
                                        ALU.subtract).then_inc(self.low_done, 1)

            def pe(self, pe):
                prenorm_pe(pe, self.n, self.norm_unit)
                products(pe, self.up, xh, xl, before=wait_x(pe, self.norm_unit))
                with pe.Fori(0, LOOPS) as i:
                    for g in range(2):
                        products(pe, self.up + 1 + g, xh, xl, i)
                        self.turn_pe(pe, g, i)
                self.turn_pe(pe, FG - 1)

                def split(k0, kn):
                    pe.wait_ge(self.low_done, (k0 + kn) // 2)
                products(pe, self.down, hh, hl, before=split)
                products(pe, self.down + 1, hh, hl)

            def act(self, act):
                prenorm_act(act, self.n, self.norm_unit, self.g0)
                stream_act(act, self.up)
                self.to_prod(act, 0)
                stream_act(act, self.up + 1)
                self.tap2_act(act, 0)
                self.to_prod(act, 1)
                self.silu_act(act, 0)
                self.high_act(act, 0)
                stream_act(act, self.up + 2)
                self.tap2_act(act, 1)
                self.to_prod(act, 2)
                self.silu_act(act, 1)
                self.high_act(act, 1)
                with act.Fori(1, LOOPS) as i:
                    for g in range(2):
                        stream_act(act, self.up + 1 + g, i)
                        self.tap2_act(act, g, i)
                        self.to_prod(act, 1 + g, i)
                        self.silu_act(act, g, i)
                        self.high_act(act, g, i)
                self.tap2_act(act, FG - 1)
                self.silu_act(act, FG - 1)
                self.high_act(act, FG - 1)
                add_act(act, self.down)

            def dve(self, dve):
                prenorm_dve(dve, self.n, self.norm_unit, self.g0)
                stream_dve(dve, self.up)
                with dve.Fori(0, LOOPS) as i:
                    for g in range(2):
                        stream_dve(dve, self.up + 1 + g, i)
                        self.taps_dve(dve, g, i)
                self.taps_dve(dve, FG - 1)
                stream_dve(dve, self.down)
                stream_dve(dve, self.down + 1)
                add_dve(dve, self.down)

            def pool(self, pool):
                prenorm_pool(pool, self.n)
                with pool.Fori(0, LOOPS) as i:
                    for g in range(2):
                        self.y_pool(pool, g, i)
                        self.low_pool(pool, g, i)
                self.y_pool(pool, FG - 1)
                self.low_pool(pool, FG - 1)

        order = []
        for i in range(2):
            if f"ffn{i}0" in stages:
                order.append(Ffn(f"ffn{i}0", g1(i, 0), ins["norm_g"][i, 1, :]))
            if i == 0 and "sc" in stages:
                order.append(ShortConv())
            if i == 1 and "gdn" in stages:
                order.append(GatedDelta())
            if f"ffn{i}1" in stages:
                order.append(Ffn(f"ffn{i}1", g1(i, 4), ins["norm_g"][i, 5, :]))

        CONSTS = 3 + 1 + 2 + 7
        if "mix" in stages:
            order.append(Mixer())
        if "ffn2" in stages:
            order.append(ConvFfn())
        left = nc.sbuf_usable_end - nc.sbuf_base
        assert left >= 0
        block = ctx.enter_context(nc.Block())

        @block.sync
        def _(sp):
            for b, part in enumerate(vec_rows):
                r = 0
                for _, rows, n in part:
                    for c in range(P // rows.shape[1]):
                        sp.dma_start(stage_rows[b][r:r + n, c * rows.shape[1]:(c + 1) * rows.shape[1]], rows).then_inc(rows_in, 16)
                    r += n
            sp.dma_start(res[:, :, :], ins["x"][0].rearrange("(b p) d -> p b d", p=P)).then_inc(res_in, 16)
            for s_ in order:
                s_.sp(sp)
            sp.wait_ge(res_ready, 4 * plan["post"])
            sp.dma_start(out[0].rearrange("(b p) d -> p b d", p=P), res[:, :, :]).then_inc(stored, 16)
            sp.wait_ge(stored, 16)

        @block.gpsimd
        def _(pool):
            pool.memset(ident[:, :], 0.0).then_inc(ident_zero, 1)
            pool.memset(ones[:, :], 1.0).then_inc(consts, 1)
            pool.memset(mhalf[:, :], -0.5).then_inc(consts, 1)
            pool.memset(minus1[:, :], -1.0).then_inc(consts, 1)
            pool.memset(upto[:, :], 1.0).then_inc(ident_zero, 1)
            pool.memset(beyond[:, :], 1.0).then_inc(ident_zero, 1)
            pool.memset(lvmask[:, :, :], 1.0).then_inc(ident_zero, 1)
            pool.wait_ge(ident_zero, 4)
            pool.affine_select(out=upto[:, :], in_=upto[:, :], compare_op=ALU.is_ge, fill=0.0, base=0,
                               pattern=[[1, P]], channel_multiplier=-1).then_inc(consts, 1)
            pool.affine_select(out=beyond[:, :], in_=beyond[:, :], compare_op=ALU.is_gt, fill=0.0, base=0,
                               pattern=[[-1, P]], channel_multiplier=1).then_inc(consts, 1)
            for l in range(7):
                b = 1 << l
                m = lvmask[:, l, :].rearrange("p (n b) -> p n b", b=b)
                pool.affine_select(out=m, in_=m, compare_op=ALU.is_ge, fill=0.0, base=0,
                                   pattern=[[-2 * b, 64 // b], [0, b]], channel_multiplier=1).then_inc(ident_zero, 1)
                pool.wait_ge(ident_zero, 5 + l)
                pool.affine_select(out=m, in_=m, compare_op=ALU.is_ge, fill=0.0, base=b - 1,
                                   pattern=[[2 * b, 64 // b], [0, b]], channel_multiplier=-1).then_inc(consts, 1)
            pool.affine_select(out=ident[:, :], in_=ident[:, :], compare_op=ALU.not_equal, fill=1.0, base=0,
                               pattern=[[-1, P]], channel_multiplier=1).then_inc(consts, 1)
            pool.wait_ge(consts, CONSTS)
            for s_ in order:
                s_.pool(pool)

        @block.scalar
        def _(act):
            act.wait_ge(consts, CONSTS)
            for b, part in enumerate(vec_rows):
                n = sum(x[2] for x in part)
                act.wait_ge(vec_tr, 5)
                nc.scalar.activation(vec[:, b * P:b * P + n], aux[b // 4][:, b % 4 * P:b % 4 * P + n], ACT.Copy).then_inc(vec_ready, 1)
            split_high(act, 0)
            split_high(act, 1)
            for s_ in order:
                s_.act(act)

        @block.vector
        def _(dve):
            dve.wait_ge(vec_ready, 5)
            dve.wait_ge(consts, CONSTS)
            split_low(dve, 0)
            split_low(dve, 1)
            for s_ in order:
                s_.dve(dve)

        @block.tensor
        def _(pe):
            pe.wait_ge(consts, CONSTS)
            pe.wait_ge(rows_in, 16 * sum(P // x[1].shape[1] for part in vec_rows for x in part))
            for b, part in enumerate(vec_rows):
                n = sum(x[2] for x in part)
                nc.tensor.transpose(aux[b // 4][:, b % 4 * P:b % 4 * P + n], stage_rows[b][0:n, :], ident[0:n, 0:n]).then_inc(vec_tr, 1)
            for s_ in order:
                s_.pe(pe)


_NAMES = ["x", "norm_g", "ffn_w_gate_up", "ffn_w_down", "sc_w_in", "sc_conv_w", "sc_w_out", "gdn_w_in",
          "gdn_conv_w", "gdn_a_log", "gdn_dt_bias", "gdn_norm_w", "gdn_w_out", "norm_mix_2", "norm_ffn_2",
          "w_in_2", "qk_gain_2", "cmp_pe_2", "cmp_w1_2", "cmp_w2_2", "rwkv_mu_2", "rwkv_w0_2", "rwkv_w_up_2",
          "rwkv_a0_2", "rwkv_a_up_2", "rwkv_g_up_2", "rwkv_k_k_2", "rwkv_k_a_2", "rwkv_r_k_2", "rwkv_ln_w_2",
          "rwkv_ln_b_2", "proj_nsa_2", "proj_rwkv_2", "w_out_2", "ffn_up_2", "ffn_conv_2", "ffn_down_2"]
STAGES = ["ffn00", "sc", "ffn01", "ffn10", "gdn", "ffn11", "mix", "ffn2"]


def kernel(**inputs):
    import concourse.bacc as bacc
    from concourse.bass_utils import run_bass_kernel_spmd

    nc = bacc.Bacc("TRN2", target_bir_lowering=False, num_devices=1)
    arrays, ins = {}, {}
    for name in _NAMES:
        a = np.ascontiguousarray(inputs[name])
        arrays[f"in_{name}"] = a
        ins[name] = nc.dram_tensor(f"in_{name}", a.shape, mybir.dt.from_np(a.dtype), kind="ExternalInput").ap()
    out = nc.dram_tensor("out", (1, SEQ, D), F32, kind="ExternalOutput").ap()
    build(nc, ins, out, STAGES)
    r = run_bass_kernel_spmd(nc, [arrays], core_ids=[0])
    return r.results[0]["out"]
```
